# Optimizing a Trainium2 kernel written in Bass

```python
import math
import jax, jax.numpy as jnp
from jax import lax
import numpy as np

D_MODEL = 1024
BATCH = 1
SEQ = 256
DEPTH = 2

N_MIXERS = 4
N_MEM = 256
HEAD_DIM = 64
MEM_HEADS = 4
MEM_WIDTH = MEM_HEADS * HEAD_DIM
MLA_HEADS = 12
MLA_Q_LORA = 384
MLA_KV_LORA = 256
MLA_NOPE = 64
MLA_ROPE = 32
MLA_V = 64
ROPE_THETA = 10000.0
Q_BLOCK = 128
A_IN = MLA_Q_LORA + MLA_KV_LORA + MLA_ROPE + MEM_WIDTH
A_OUT = MLA_HEADS * MLA_V + MEM_WIDTH
DIL_GROUPS = ((128, 1), (512, 4), (2048, 16))
DIL_HEADS = 8
DIL_BLOCK = 64
DIL_QKV = len(DIL_GROUPS) * 3 * DIL_HEADS * HEAD_DIM
B_IN = DIL_QKV + MEM_WIDTH
B_OUT = DIL_HEADS * HEAD_DIM + MEM_WIDTH
ALIBI_MAX = 8.0
CONV_CH = 768
CONV_WIDTH = 31
C_IN = 2 * CONV_CH + MEM_WIDTH
C_OUT = CONV_CH + MEM_WIDTH
SC_CH = 768
SC_WIDTH = 3
D_IN = 3 * SC_CH + MEM_WIDTH
D_OUT = SC_CH + MEM_WIDTH
D_FF = 2816
EPS = 1e-6
NEG = -1e30

kernel_name = "hybrid_interleaved_mla_dilated_conformer_shortconv_encoder"

def _n_uses(m):
    return len(range(m, DEPTH, N_MIXERS))

def rms_norm(x, g):
    xf = x.astype(jnp.float32)
    y = xf * lax.rsqrt(jnp.mean(xf * xf, axis=-1, keepdims=True) + EPS)
    return (y * g.astype(jnp.float32)).astype(x.dtype)

def layer_norm(x, g, b):
    xf = x.astype(jnp.float32)
    mu = jnp.mean(xf, axis=-1, keepdims=True)
    var = jnp.mean(jnp.square(xf - mu), axis=-1, keepdims=True)
    y = (xf - mu) * lax.rsqrt(var + EPS)
    return (y * g.astype(jnp.float32) + b.astype(jnp.float32)).astype(x.dtype)

def swiglu(h, wg, wu, wd):
    return jnp.einsum('bsf,fd->bsd', jax.nn.silu(h @ wg) * (h @ wu), wd)

def depthwise_conv(u, w):
    width, ch = w.shape
    return lax.conv_general_dilated(
        u, w[:, None, :].astype(u.dtype), window_strides=(1,),
        padding=[(width // 2, width // 2)],
        dimension_numbers=('NWC', 'WIO', 'NWC'), feature_group_count=ch)

def alibi_slopes(n):
    return 2.0 ** (-ALIBI_MAX * (jnp.arange(n, dtype=jnp.float32) + 1.0) / n)

def apply_rope(t, cos, sin):
    if t.ndim == 4:
        cos, sin = cos[:, :, None, :], sin[:, :, None, :]
    half = t.shape[-1] // 2
    tf = t.astype(jnp.float32)
    t1, t2 = tf[..., :half], tf[..., half:]
    return jnp.concatenate([t1 * cos - t2 * sin, t1 * sin + t2 * cos], axis=-1).astype(t.dtype)

def memory_attention(q_mem, mem_n, w_kv):
    bsz, seq, _ = q_mem.shape
    kv = (mem_n @ w_kv).reshape(bsz, mem_n.shape[1], 2, MEM_HEADS, HEAD_DIM)
    k, v = kv[:, :, 0], kv[:, :, 1]
    q = q_mem.reshape(bsz, seq, MEM_HEADS, HEAD_DIM)
    s = jnp.einsum('bshd,bnhd->bhsn', q, k).astype(jnp.float32) * HEAD_DIM ** -0.5
    p = jax.nn.softmax(s, axis=-1).astype(v.dtype)
    return jnp.einsum('bhsn,bnhd->bshd', p, v).reshape(bsz, seq, MEM_WIDTH)

def mla_mixer(h, positions, w_in, q_g, kv_g, w_uq, w_ukv):
    bsz, seq, _ = h.shape
    z = h @ w_in
    o1 = MLA_Q_LORA
    o2 = o1 + MLA_KV_LORA
    o3 = o2 + MLA_ROPE
    c_q, c_kv, k_r, q_mem = z[..., :o1], z[..., o1:o2], z[..., o2:o3], z[..., o3:]
    half = MLA_ROPE // 2
    inv = ROPE_THETA ** (-jnp.arange(half, dtype=jnp.float32) / half)
    ang = positions.astype(jnp.float32)[..., None] * inv
    cos, sin = jnp.cos(ang), jnp.sin(ang)
    q = (rms_norm(c_q, q_g) @ w_uq).reshape(bsz, seq, MLA_HEADS, MLA_NOPE + MLA_ROPE)
    q_n, q_r = q[..., :MLA_NOPE], apply_rope(q[..., MLA_NOPE:], cos, sin)
    kv = (rms_norm(c_kv, kv_g) @ w_ukv).reshape(bsz, seq, MLA_HEADS, MLA_NOPE + MLA_V)
    k_n, v = kv[..., :MLA_NOPE], kv[..., MLA_NOPE:]
    k_r = apply_rope(k_r, cos, sin)
    scale = (MLA_NOPE + MLA_ROPE) ** -0.5
    nb = seq // Q_BLOCK
    qn_b = q_n.reshape(bsz, nb, Q_BLOCK, MLA_HEADS, MLA_NOPE).transpose(1, 0, 2, 3, 4)
    qr_b = q_r.reshape(bsz, nb, Q_BLOCK, MLA_HEADS, MLA_ROPE).transpose(1, 0, 2, 3, 4)

    def block(args):
        qn, qr = args
        s = (jnp.einsum('bqhd,bkhd->bhqk', qn, k_n)
             + jnp.einsum('bqhr,bkr->bhqk', qr, k_r)).astype(jnp.float32) * scale
        p = jax.nn.softmax(s, axis=-1).astype(v.dtype)
        return jnp.einsum('bhqk,bkhd->bqhd', p, v)

    o = lax.map(block, (qn_b, qr_b))
    o = o.transpose(1, 0, 2, 3, 4).reshape(bsz, seq, MLA_HEADS * MLA_V)
    return o, q_mem

def dilated_group(q, k, v, dilation, half, slopes):
    bsz, seq, nh, dh = q.shape
    sub_len = seq // dilation
    nb = -(-sub_len // DIL_BLOCK)
    lp = nb * DIL_BLOCK

    def sub(t):
        return t.reshape(bsz, sub_len, dilation, nh, dh).transpose(0, 2, 1, 3, 4)

    qs = jnp.pad(sub(q), ((0, 0), (0, 0), (0, lp - sub_len), (0, 0), (0, 0)))
    qs = qs.reshape(bsz, dilation, nb, DIL_BLOCK, nh, dh)

    def kv_blocks(t):
        t = jnp.pad(sub(t), ((0, 0), (0, 0), (DIL_BLOCK, lp - sub_len + DIL_BLOCK), (0, 0), (0, 0)))
        t = t.reshape(bsz, dilation, nb + 2, DIL_BLOCK, nh, dh)
        return jnp.concatenate([t[:, :, :-2], t[:, :, 1:-1], t[:, :, 2:]], axis=3)

    kb, vb = kv_blocks(k), kv_blocks(v)
    qi = jnp.arange(DIL_BLOCK)
    kj = jnp.arange(3 * DIL_BLOCK)
    rel = kj[None, :] - DIL_BLOCK - qi[:, None]
    key_idx = jnp.arange(nb)[:, None] * DIL_BLOCK - DIL_BLOCK + kj[None, :]
    mask = (jnp.abs(rel) <= half)[None] & ((key_idx >= 0) & (key_idx < sub_len))[:, None, :]
    dist = (jnp.abs(rel) * dilation).astype(jnp.float32)
    s = jnp.einsum('brnqhd,brnkhd->brnhqk', qs, kb).astype(jnp.float32) * dh ** -0.5
    s = s - slopes[:, None, None] * dist
    s = jnp.where(mask[:, None], s, NEG)
    lse = jax.nn.logsumexp(s, axis=-1)
    p = jnp.exp(s - lse[..., None]).astype(v.dtype)
    o = jnp.einsum('brnhqk,brnkhd->brnqhd', p, vb)
    o = o.reshape(bsz, dilation, lp, nh, dh)[:, :, :sub_len]
    o = o.transpose(0, 2, 1, 3, 4).reshape(bsz, seq, nh, dh)
    lse = lse.transpose(0, 1, 2, 4, 3).reshape(bsz, dilation, lp, nh)[:, :, :sub_len]
    lse = lse.transpose(0, 2, 1, 3).reshape(bsz, seq, nh)
    return o, lse

def dilated_mixer(h, w_in):
    bsz, seq, _ = h.shape
    z = h @ w_in
    n_g = len(DIL_GROUPS)
    zd = z[..., :DIL_QKV].reshape(bsz, seq, n_g, 3, DIL_HEADS, HEAD_DIM)
    q_mem = z[..., DIL_QKV:]
    slopes = alibi_slopes(n_g * DIL_HEADS).reshape(n_g, DIL_HEADS)
    outs, lses = [], []
    for g, (window, dilation) in enumerate(DIL_GROUPS):
        o, l = dilated_group(zd[:, :, g, 0], zd[:, :, g, 1], zd[:, :, g, 2],
                             dilation, window // (2 * dilation), slopes[g])
        outs.append(o)
        lses.append(l)
    wts = jax.nn.softmax(jnp.stack(lses, axis=0), axis=0)
    o = jnp.einsum('gbsh,gbshd->bshd', wts.astype(outs[0].dtype), jnp.stack(outs, axis=0))
    return o.reshape(bsz, seq, DIL_HEADS * HEAD_DIM), q_mem

def conformer_conv_mixer(h, w_in, conv_w, conv_b, ln_g, ln_b):
    z = h @ w_in
    a, gate, q_mem = z[..., :CONV_CH], z[..., CONV_CH:2 * CONV_CH], z[..., 2 * CONV_CH:]
    u = a * jax.nn.sigmoid(gate)
    u = depthwise_conv(u, conv_w) + conv_b
    u = jax.nn.silu(layer_norm(u, ln_g, ln_b))
    return u, q_mem

def short_conv_mixer(h, w_in, conv_w):
    z = h @ w_in
    bg, cg = z[..., :SC_CH], z[..., SC_CH:2 * SC_CH]
    hx, q_mem = z[..., 2 * SC_CH:3 * SC_CH], z[..., 3 * SC_CH:]
    return bg * depthwise_conv(cg * hx, conv_w), q_mem

def setup_inputs(seed: int = 0) -> dict:
    key = jax.random.key(seed)
    ks = jax.random.split(key, 32)
    f32 = jnp.float32

    def w(k, shape, fan_in):
        return jax.random.normal(k, shape, f32) * fan_in ** -0.5

    def gain(k, shape):
        return 1.0 + 0.05 * jax.random.normal(k, shape, f32)

    na, nb_, nc, nd = _n_uses(0), _n_uses(1), _n_uses(2), _n_uses(3)
    offset = jax.random.randint(ks[2], (BATCH, 1), 0, 4096, dtype=jnp.int32)
    positions = offset + jnp.arange(SEQ, dtype=jnp.int32)[None, :]
    return {
        "x": jax.random.normal(ks[0], (BATCH, SEQ, D_MODEL), f32),
        "mem": jax.random.normal(ks[1], (BATCH, N_MEM, D_MODEL), f32),
        "positions": positions,
        "norm_g": gain(ks[3], (DEPTH, 7, D_MODEL)),
        "ffn_w_gate": w(ks[4], (DEPTH, 2, D_MODEL, D_FF), D_MODEL),
        "ffn_w_up": w(ks[5], (DEPTH, 2, D_MODEL, D_FF), D_MODEL),
        "ffn_w_down": w(ks[6], (DEPTH, 2, D_FF, D_MODEL), D_FF),
        "mem_w_kv": w(ks[7], (DEPTH, D_MODEL, 2 * MEM_WIDTH), D_MODEL),
        "a_w_in": w(ks[8], (na, D_MODEL, A_IN), D_MODEL),
        "a_q_norm": gain(ks[9], (na, MLA_Q_LORA)),
        "a_kv_norm": gain(ks[10], (na, MLA_KV_LORA)),
        "a_w_uq": w(ks[11], (na, MLA_Q_LORA, MLA_HEADS * (MLA_NOPE + MLA_ROPE)), MLA_Q_LORA),
        "a_w_ukv": w(ks[12], (na, MLA_KV_LORA, MLA_HEADS * (MLA_NOPE + MLA_V)), MLA_KV_LORA),
        "a_w_out": w(ks[13], (na, A_OUT, D_MODEL), A_OUT),
        "b_w_in": w(ks[14], (nb_, D_MODEL, B_IN), D_MODEL),
        "b_w_out": w(ks[15], (nb_, B_OUT, D_MODEL), B_OUT),
        "c_w_in": w(ks[16], (nc, D_MODEL, C_IN), D_MODEL),
        "c_conv_w": w(ks[17], (nc, CONV_WIDTH, CONV_CH), CONV_WIDTH),
        "c_conv_b": 0.02 * jax.random.normal(ks[18], (nc, CONV_CH), f32),
        "c_ln_g": gain(ks[19], (nc, CONV_CH)),
        "c_ln_b": 0.02 * jax.random.normal(ks[20], (nc, CONV_CH), f32),
        "c_w_out": w(ks[21], (nc, C_OUT, D_MODEL), C_OUT),
        "d_w_in": w(ks[22], (nd, D_MODEL, D_IN), D_MODEL),
        "d_conv_w": w(ks[23], (nd, SC_WIDTH, SC_CH), SC_WIDTH),
        "d_w_out": w(ks[24], (nd, D_OUT, D_MODEL), D_OUT),
    }

def reference(x, mem, positions, norm_g, ffn_w_gate, ffn_w_up, ffn_w_down, mem_w_kv,
              a_w_in, a_q_norm, a_kv_norm, a_w_uq, a_w_ukv, a_w_out,
              b_w_in, b_w_out,
              c_w_in, c_conv_w, c_conv_b, c_ln_g, c_ln_b, c_w_out,
              d_w_in, d_conv_w, d_w_out):
    for i in range(DEPTH):
        g = norm_g[i]
        h = rms_norm(x, g[0])
        x = x + 0.5 * rms_norm(swiglu(h, ffn_w_gate[i, 0], ffn_w_up[i, 0], ffn_w_down[i, 0]), g[1])
        h = rms_norm(x, g[2])
        m, j = i % N_MIXERS, i // N_MIXERS
        if m == 0:
            o, q_mem = mla_mixer(h, positions, a_w_in[j], a_q_norm[j], a_kv_norm[j], a_w_uq[j], a_w_ukv[j])
            w_out = a_w_out[j]
        elif m == 1:
            o, q_mem = dilated_mixer(h, b_w_in[j])
            w_out = b_w_out[j]
        elif m == 2:
            o, q_mem = conformer_conv_mixer(h, c_w_in[j], c_conv_w[j], c_conv_b[j], c_ln_g[j], c_ln_b[j])
            w_out = c_w_out[j]
        else:
            o, q_mem = short_conv_mixer(h, d_w_in[j], d_conv_w[j])
            w_out = d_w_out[j]
        mo = memory_attention(q_mem, rms_norm(mem, g[6]), mem_w_kv[i])
        y = jnp.concatenate([o, mo], axis=-1) @ w_out
        x = x + rms_norm(y, g[3])
        h = rms_norm(x, g[4])
        x = x + 0.5 * rms_norm(swiglu(h, ffn_w_gate[i, 1], ffn_w_up[i, 1], ffn_w_down[i, 1]), g[5])
    return x


_drawn_inputs = setup_inputs


def setup_inputs(seed=0):
    import zlib

    import numpy as np

    out = dict(_drawn_inputs(seed))
    spreads = {}
    factors = {}
    for name, (base, spread) in spreads.items():
        noise = np.random.default_rng([zlib.crc32(name.encode()), seed]).standard_normal(out[name].shape)
        drawn = base * np.exp(spread * noise) if base else spread * noise
        out[name] = __import__('jax').numpy.asarray(drawn.astype(out[name].dtype))
    for name, factor in factors.items():
        out[name] = (out[name] * factor).astype(out[name].dtype)
    return out
```

```python
from contextlib import ExitStack

import numpy as np
import concourse.bass as bass
from concourse import mybir

F32 = mybir.dt.float32
F32R = mybir.dt.float32r
I32 = mybir.dt.int32
ALU = mybir.AluOpType
ACT = mybir.ActivationFunctionType
AX_X = mybir.AxisListType.X

P = 128
D = 1024
KT = D // P
SEQ = 256
NT = SEQ // P
NMEM = 256
DFF = 2816
FT = DFF // P
EPS = 1e-6
HD = 64
MEM_HEADS = 4
MLA_HEADS = 12
NOPE, ROPE = 64, 32
QK = NOPE + ROPE
QL, KVL = 384, 256
DIL_HEADS = 8
GROUPS = ((128, 1), (512, 4), (2048, 16))
CLASSES = 4
ALIBI_STEP = 2.0 ** (-8.0 / 24)
MASKED = 1e30

PIECE = 2048
RING = 3
LOOKAHEAD = 2
FFN_PIECES = FT + FT // 2
MIX0_PIECES = 2 + 4 + 2 + 2 + 4
MIX1_PIECES = 1 + 18 + 3
FILLERS = (0, 2, 1, 1, 0, 0)
COUNTS = (FFN_PIECES, MIX0_PIECES, FFN_PIECES + 1, FFN_PIECES + 1, MIX1_PIECES, FFN_PIECES)
BASES = tuple(sum(COUNTS[:s]) for s in range(len(COUNTS)))
PIECES = sum(COUNTS)
FFNS = {0: 0, 2: 1, 3: 2, 5: 3}
Y_BANK = (0, 0, 4, 0, 0, 4)
X_BANK = (0, 4, 4, 0, 4, 4)
GU_BANK = {0: 4, 2: 0, 3: 4, 5: 0}
S_BANK, PT_BANK, O_BANK = 4, 6, 7
HALF_PI = float(np.pi / 2)
TP1 = float(np.float32(6.28125))
TP2 = float(np.float32(np.float64(2 * np.pi - TP1) // 2.0 ** -21 * 2.0 ** -21))
TP3 = float(2 * np.pi - TP1 - TP2)
ROUND = float(1.5 * 2 ** 23)

STEPS1 = []
for _p in range(4):
    STEPS1 += [("qk", g, _p) for g in range(3)] + [("v01", 0, _p)] + ([("v2", 2, _p)] if _p % 2 == 0 else [])
TICKS1 = [(0, 0, 0, 1), (0, 1, 0, 1), (1, 0, 1, 0), (1, 0, 1, 0), (0, 1, 0, 0), (0, 1, 0, 0),
          (0, 1, 0, 0), (1, 0, 1, 0), (0, 0, 1, 0), (0, 1, 0, 0), (0, 1, 0, 0), (0, 1, 0, 0),
          (0, 0, 1, 0), (0, 1, 0, 0), (0, 1, 0, 0), (0, 1, 0, 0), (0, 0, 0, 0), (0, 1, 1, 1)]
TICKS1_OUT = [(1, 1, 1, 1), (0, 0, 0, 0), (0, 0, 0, 0)]
TICKS0 = [(1, 1, 1, 1, 0, 0), (1, 0, 1, 0, 1, 0), (0, 1, 1, 1, 1, 2), (1, 1, 1, 1, 1, 1)]
TICKS0_OUT = [(1, 1, 1, 1), (1, 1, 1, 2), (2, 2, 2, 0), (0, 0, 0, 0)]

C_ID, C_DIST, C_INV = 0, P, P + 2 * 512
C_N = C_INV + 16
G_Q = 2 * 7 * KT
G_KV = G_Q + QL // P
G_N = G_KV + KVL // P


def build(nc, x_in, mem_in, pos_in, stream, gcols, grows, consts, out):
    with ExitStack() as ctx:
        def sb(name, shape, dt=F32):
            return ctx.enter_context(nc.sbuf_tensor(name, shape, dt))

        def sem(name):
            return ctx.enter_context(nc.semaphore(name))

        raw = sb("raw", [P, RING, PIECE])
        w_hi = sb("w_hi", [P, RING, PIECE], F32R)
        w_lo = sb("w_lo", [P, RING, PIECE], F32R)
        x = sb("x", [P, NT, D])
        work = sb("work", [P, NT, D])
        junk = sb("junk", [P, D])
        h_hi = sb("h_hi", [P, KT, SEQ], F32R)
        h_lo = sb("h_lo", [P, KT, SEQ], F32R)
        memT = sb("memT", [P, KT, NMEM])
        m_hi = sb("m_hi", [P, KT, NMEM], F32R)
        m_lo = sb("m_lo", [P, KT, NMEM], F32R)
        a_hi = sb("a_hi", [P, 4, SEQ], F32R)
        a_lo = sb("a_lo", [P, 4, SEQ], F32R)
        kmT = sb("kmT", [P, 2, NMEM])
        vm = sb("vm", [P, 2, MEM_HEADS * HD])
        qmT = sb("qmT", [P, 2, SEQ])
        g_row = sb("g_row", [P, D])
        cst = sb("cst", [P, C_N])
        gcol = sb("gcol", [P, G_N])
        posi = sb("posi", [P, NT], I32)
        posf = sb("posf", [P, NT])
        ang = sb("ang", [P, NT, 6, 16])
        cc = sb("cc", [P, NT, 32])
        ss = sb("ss", [P, NT, 32])
        kr = sb("kr", [P, NT, ROPE])
        rt = sb("rt", [P, 2, 6 * ROPE])
        stat_ms = sb("stat_ms", [P, 32])
        stat_ve = sb("stat_ve", [P, 32])
        rstd = sb("rstd", [P, 32])
        neg_half = sb("neg_half", [P, 1])
        NU = 32 + 24
        neg_max = sb("neg_max", [P, NU])
        den = sb("den", [P, NU])
        rden = sb("rden", [P, NU])
        MIX = 3 * 3072 + 3 * 1024
        mix = sb("mix", [P, MIX])
        ps = ctx.enter_context(nc.psum_tensor("ps", [P, 8, 512], F32))

        def part(off, *shape):
            n = int(np.prod(shape))
            v = mix[:, off:off + n]
            names = "abcd"[:len(shape)]
            kw = {c: s for c, s in zip(names[1:], shape[1:])}
            return v.rearrange(f"p ({' '.join(names)}) -> p {' '.join(names)}", **kw) if len(shape) > 1 else v

        silu_g = part(0, 2, SEQ)
        act_f = part(512, 2, SEQ)
        tok = part(0, 4, 6, QK)
        v0 = part(2304, NT, MLA_HEADS, HD)
        qT = part(3840, MLA_HEADS, SEQ)
        kT = part(6912, MLA_HEADS, SEQ)
        zc = part(9984, NT, QL + KVL)
        q1T = part(0, 3, 4, SEQ)
        k1T = part(3072, 3, 4, SEQ)
        v1 = part(6144, 3, NT, DIL_HEADS * HD)
        sbias = part(9216, 2, 512)
        prob = part(10240, 2, 512)
        probT = part(11264, 2, 512)

        ident = cst[:, C_ID:C_ID + P]
        dist = cst[:, C_DIST:C_DIST + 1024].rearrange("p (t n) -> p t n", t=2)
        inv_freq = cst[:, C_INV:C_INV + 16]

        w_landed = [sem(f"w_landed{i}") for i in range(RING)]
        hi_ready, lo_ready = sem("hi_ready"), sem("lo_ready")
        w_used = sem("w_used")
        ident_in, consts_in, gcol_in, mem_in_s, pos_s = (sem(n) for n in (
            "ident_in", "consts_in", "gcol_in", "mem_landed", "pos_landed"))
        x_in_s = [sem(f"x_landed{t}") for t in range(NT)]
        g_row_in = sem("g_row_in")
        half_set, rope_step, rope_sin, rope_ready = (sem(n) for n in (
            "half_set", "rope_step", "rope_sin", "rope_ready"))
        ms_ready, ve_ready, rstd_ready = sem("ms_ready"), sem("ve_ready"), sem("rstd_ready")
        x_ready, xn_ready, xT_done, h_hi_ready, h_lo_ready = (sem(n) for n in (
            "x_ready", "xn_ready", "xT_done", "h_hi_ready", "h_lo_ready"))
        y_done, yg_done = sem("y_done"), sem("yg_done")
        memn_ready, memT_done, memT_ready = sem("memn_ready"), sem("memT_done"), sem("memT_ready")
        m_hi_ready, m_lo_ready, km_ready, vm_ready, qm_ready = (sem(n) for n in (
            "m_hi_ready", "m_lo_ready", "km_ready", "vm_ready", "qm_ready"))
        g_done, silu_done, a_done, a_hi_ready, a_lo_ready = (sem(n) for n in (
            "g_done", "silu_done", "a_done", "a_hi_ready", "a_lo_ready"))
        lat_ready, latT_done, lat_hi, lat_lo = (sem(n) for n in ("lat_ready", "latT_done", "lat_hi", "lat_lo"))
        kr_step, kr_ready, up_done, tok_a, tok_d, tok_p, rope_tmp = (sem(n) for n in (
            "kr_step", "kr_ready", "up_done", "tok_a", "tok_d", "tok_p", "rope_tmp"))
        tokT_done, tokT_a, tokT_d = sem("tokT_done"), sem("tokT_a"), sem("tokT_d")
        z1_a, z1_d = sem("z1_a"), sem("z1_d")
        s_done, sb_done, max_done, p_done, pT_done, pT_ready, rden_done, o_done, o_ready = (
            sem(n) for n in ("s_done", "sb_done", "max_done", "p_done", "pT_done", "pT_ready",
                             "rden_done", "o_done", "o_ready"))
        oT_done, oh_hi, oh_lo = sem("oT_done"), sem("oh_hi"), sem("oh_lo")
        out_done = sem("out_done")

        block = ctx.enter_context(nc.Block())

        def gain(layer, r, kt):
            c = (layer * 7 + r) * KT + kt
            return gcol[:, c:c + 1]

        UNITS0 = [("mem", h, t) for h in range(MEM_HEADS) for t in range(NT)] + \
                 [("mla", h, t) for h in range(MLA_HEADS) for t in range(NT)]
        UNITS1 = [("mem", h, t) for h in range(MEM_HEADS) for t in range(NT)] + \
                 [("dil", h, t) for h in range(DIL_HEADS) for t in range(NT)]
        UNITS = {1: (0, UNITS0), 4: (len(UNITS0), UNITS1)}
        OWN = {1: MLA_HEADS * HD, 4: DIL_HEADS * HD}

        SQUARES = []
        SQUARES += [(kind, 0, t) for kind in ("x", "mem") for t in range(NT)]
        for s in range(len(BASES)):
            SQUARES += [(c, s, t) for t in range(NT) for c in ("cq", "ckv")] if s == 1 else []
            for t in range(NT):
                SQUARES += [("y", s, t)] + ([("x", s + 1, t)] if s < 5 else [])

        def root_of(key):
            k = SQUARES.index(key)
            return rstd[:, k:k + 1], k + 1

        def y_of(s, t):
            return (y_done, s + 1) if t == 0 else (w_used, BASES[s] + COUNTS[s])

        def up_of(c):
            return (up_done, c // 2 + 1) if c % 2 == 0 else (w_used, BASES[1] + 7 + c // 2)

        def chunk(c):
            return c % 4 < 2, c // 4, c % 2

        def out_groups(s):
            n = OWN[s] // P
            return [(n, 2 * MEM_HEADS)] + [(k, 2 * MEM_HEADS + 4 * (k + 2)) for k in range(0, n, 2)]

        def value_rows(kind, p, b):
            if kind == "v01":
                return (v1[:, 0:2, :, p * P:(p + 1) * P].rearrange("p g t n -> p t g n"),
                        ps[:, b, :].rearrange("p (t g n) -> p t g n", t=NT, g=2))
            return v1[:, 2, :, p * P:(p + 2) * P], ps[:, b, :].rearrange("p (t n) -> p t n", t=NT)

        def evacuated(k):
            count = sum(2 if STEPS1[i][0] == "qk" else 1 for i in range(k % 2, k + 1, 2))
            return (z1_a, z1_d)[k % 2], count

        def o_cols(s, kind, h):
            return (OWN[s] if kind == "mem" else 0) + h * HD

        @block.sync
        def _(sp):
            for t in range(NT):
                sp.dma_start(x[:, t, :], x_in[t]).then_inc(x_in_s[t], 16)
            sp.dma_start(cst[:, 0:P], consts[:, 0:P]).then_inc(ident_in, 16)
            sp.dma_start(gcol[:, :], gcols).then_inc(gcol_in, 16)

            def load(i, slot, wait):
                if wait:
                    sp.wait_ge(lo_ready, 2 * i - 2 * (RING - 1))
                sp.dma_start(raw[:, slot, :], stream[i]).then_inc(w_landed[slot], 16)

            for i in range(RING):
                load(i, i, False)
            sp.dma_start(posi[:, :], pos_in).then_inc(pos_s, 16)
            sp.dma_start(cst[:, P:C_N], consts[:, P:C_N]).then_inc(consts_in, 16)
            sp.wait_ge(xT_done, NT)
            for t in range(NT):
                sp.dma_start(work[:, t, :], mem_in[t]).then_inc(mem_in_s, 16)
            for s, base in enumerate(BASES):
                a = base + 6
                start = RING if s == 0 else BASES[s - 1] + 6
                full = start + (a - start) // RING * RING
                with sp.Fori(start, full - RING + 1, RING) as i:
                    for j in range(RING):
                        load(i + j, (start + j) % RING, True)
                for i in range(full, a):
                    load(i, i % RING, True)
                if s > 0:
                    sp.wait_ge(yg_done, NT * s)
                sp.dma_start(g_row[:, :], grows[s:s + 1, :].broadcast_to([P, D])).then_inc(g_row_in, 16)
            start = BASES[-1] + 6
            full = start + (PIECES - start) // RING * RING
            with sp.Fori(start, full - RING + 1, RING) as i:
                for j in range(RING):
                    load(i + j, (start + j) % RING, True)
            for i in range(full, PIECES):
                load(i, i % RING, True)
            for t in range(NT):
                sp.wait_ge(x_ready, NT * (len(BASES) - 1) + t + 1)
                sp.dma_start(out[t], x[:, t, :]).then_inc(out_done, 16)
            sp.wait_ge(out_done, 16 * NT)

        @block.gpsimd
        def _(pool):
            pool.memset(neg_half[:, :], -0.5).then_inc(half_set, 1)
            pool.wait_ge(half_set, 1)
            steps = [0]

            def link(ins):
                steps[0] += 1
                ins.then_inc(rope_step, 1)
                pool.wait_ge(rope_step, steps[0])

            def rotary_angles():
                pool.wait_ge(pos_s, 16)
                pool.wait_ge(consts_in, 16)
                link(pool.tensor_copy(posf[:, :], posi[:, :]))
                A, K1, K0, T, B, C = (ang[:, :, i, :] for i in range(6))
                for t in range(NT):
                    link(pool.tensor_scalar(A[:, t, :], inv_freq, posf[:, t:t + 1], None, ALU.mult))
                link(pool.tensor_scalar(T, A, 1.0 / (2 * np.pi), ROUND, ALU.mult, ALU.add))
                link(pool.tensor_scalar(T, T, -ROUND, None, ALU.add))
                link(pool.tensor_scalar(K1, T, 1.0 / 4096, ROUND, ALU.mult, ALU.add))
                link(pool.tensor_scalar(K1, K1, -ROUND, 4096.0, ALU.add, ALU.mult))
                link(pool.tensor_tensor(K0, T, K1, ALU.subtract))
                for part_of in (TP1, TP2, TP3):
                    for K in (K1, K0):
                        link(pool.tensor_scalar(B, K, -part_of, None, ALU.mult))
                        link(pool.tensor_tensor(A, A, B, ALU.add))
                pi = float(np.float32(np.pi)) - 1e-6
                link(pool.tensor_scalar(A, A, pi, -pi, ALU.min, ALU.max))
                link(pool.tensor_scalar(B, A, 0.0, 2.0, ALU.is_ge, ALU.mult))
                link(pool.tensor_scalar(B, B, -1.0, None, ALU.add))
                link(pool.tensor_tensor(B, A, B, ALU.mult))
                link(pool.tensor_scalar(C, B, -1.0, HALF_PI, ALU.mult, ALU.add))
                assert steps[0] == ROPE_STEPS
                pool.wait_ge(rope_sin, 2)
                pool.tensor_copy(cc[:, :, 16:32], cc[:, :, 0:16]).then_inc(rope_ready, 1)
                pool.tensor_scalar(ss[:, :, 0:16], ss[:, :, 16:32], -1.0, None, ALU.mult).then_inc(rope_ready, 1)

            for k, (kind, s, t) in enumerate(SQUARES):
                factor = 4.0 if kind == "y" and s in FFNS else 1.0
                pool.wait_ge(ms_ready, k + 1)
                pool.tensor_scalar(stat_ve[:, k:k + 1], stat_ms[:, k:k + 1], EPS, factor,
                                   ALU.add, ALU.mult).then_inc(ve_ready, 1)
                pool.wait_ge(ve_ready, k + 1)
                pool.tensor_tensor(rstd[:, k:k + 1], stat_ve[:, k:k + 1], neg_half[:, 0:1],
                                   ALU.pow).then_inc(rstd_ready, 1)
                if (kind, t) == ("mem", NT - 1):
                    rotary_angles()
                if (kind, t) == ("ckv", NT - 1):
                    pool.wait_ge(kr_ready, 1)
                    for c in (2, 3, 6, 7):
                        if c >= 4:
                            pool.wait_ge(tokT_done, c - 3)
                        pool.tensor_copy(tok[:, c % 4, :, NOPE:QK],
                                         kr[:, c % 2:c % 2 + 1, :].broadcast_to([P, 6, ROPE])).then_inc(tok_p, 1)

        @block.scalar
        def _(act):
            def mean_square(key, src, scale):
                k = SQUARES.index(key)
                if k:
                    act.wait_ge(ms_ready, k)
                n = int(np.prod(src.shape[1:]))
                act.activation(junk[:, 0:n], src, ACT.Square, scale=scale,
                               accum_out=stat_ms[:, k:k + 1]).then_inc(ms_ready, 1)

            def split(n, slot, count, half=None):
                if half != 1:
                    act.wait_ge(w_landed[slot], 16 * count)
                    if not isinstance(n, int) or n >= RING:
                        act.wait_ge(w_used, n - (RING - 1))
                c = slice(0, PIECE) if half is None else slice(half * PIECE // 2, (half + 1) * PIECE // 2)
                act.activation(w_hi[:, slot, c], raw[:, slot, c],
                               ACT.Copy).then_inc(hi_ready, 2 if half is None else 1)

            def ahead(n, half=None):
                n += LOOKAHEAD
                if n < PIECES:
                    split(n, n % RING, n // RING + 1, half)

            def mean_square_x(s, t):
                act.wait_ge(*((x_in_s[t], 16) if s == 0 else (x_ready, NT * (s - 1) + t + 1)))
                mean_square(("x", s, t), x[:, t, :], 1.0 / 32)

            def pre_norm(s):
                if s == 0:
                    act.wait_ge(gcol_in, 16)
                act.wait_ge(xT_done, NT * s + NT)
                for kt in range(KT):
                    act.activation(h_hi[:, kt, :], ps[:, X_BANK[s] + kt // 2, kt % 2 * SEQ:(kt % 2 + 1) * SEQ],
                                   ACT.Copy, scale=gain(s // 3, 2 * (s % 3), kt)).then_inc(h_hi_ready, 1)

            def post_norm(s):
                for t in range(NT):
                    act.wait_ge(*y_of(s, t))
                    b = Y_BANK[s] + 2 * t
                    mean_square(("y", s, t), ps[:, b:b + 2, :], 1.0 / 32)
                    if t == NT - 1:
                        ahead(BASES[s] + COUNTS[s] - 1)
                    if s < 5:
                        mean_square_x(s + 1, t)

            def silu(s, F, f):
                act.wait_ge(g_done, F + 1)
                if not isinstance(F, int) or F >= 2:
                    act.wait_ge(a_done, F - 1)
                act.activation(silu_g[:, f % 2, :], ps[:, GU_BANK[s] + f % 2, 0:SEQ], ACT.Silu).then_inc(silu_done, 1)

            def act_hi(F, f, slot, used):
                act.wait_ge(a_done, F + 1)
                if used is not None:
                    act.wait_ge(w_used, used)
                act.activation(a_hi[:, slot, :], act_f[:, f % 2, :], ACT.Copy).then_inc(a_hi_ready, 1)

            def mem_norm():
                for t in range(NT):
                    act.wait_ge(mem_in_s, 16 * NT)
                    mean_square(("mem", 0, t), work[:, t, :], 1.0 / 32)
                for b in range(KT // 2):
                    act.wait_ge(memT_done, 1)
                    act.activation(memT[:, 2 * b:2 * b + 2, :].rearrange("p a b -> p (a b)"), ps[:, b, :],
                                   ACT.Copy).then_inc(memT_ready, 1)

            def mem_gain(layer):
                act.wait_ge(memT_ready, KT // 2)
                for kt in range(KT):
                    act.activation(m_hi[:, kt, :], memT[:, kt, :], ACT.Copy,
                                   scale=gain(layer, 6, kt)).then_inc(m_hi_ready, 1)

            def ffn(s):
                base, F0 = BASES[s] + FILLERS[s], FT * FFNS[s]
                ahead(base)
                silu(s, F0, 0)
                if s == 0:
                    mem_norm()
                act_hi(F0, 0, 0, None)
                ahead(base + 1)
                silu(s, F0 + 1, 1)
                if s == 0:
                    mem_gain(0)
                    act.wait_ge(rope_step, ROPE_STEPS)
                    act.activation(ss[:, :, 16:32], ang[:, :, 0, :], ACT.Sin).then_inc(rope_sin, 1)
                    act.activation(cc[:, :, 0:16], ang[:, :, 5, :], ACT.Sin).then_inc(rope_sin, 1)

                def period(c):
                    n = base + 3 * c - 1
                    F = F0 + 2 * c
                    r = (base - 1 + LOOKAHEAD) % RING
                    q = (base - 1 + LOOKAHEAD) // RING
                    act_hi(F - 1, 1, 1, None)
                    split(n + 2, r, c + q + 1)
                    silu(s, F, 0)
                    split(n + 3, (r + 1) % RING, c + q + 1 + (r + 1) // RING)
                    act_hi(F, 0, 0, n + 2)
                    split(n + 4, (r + 2) % RING, c + q + 1 + (r + 2) // RING)
                    silu(s, F + 1, 1)

                period(1)
                last = FT // 2 - 1
                with act.Fori(2, last) as c:
                    period(c)
                n = base + 3 * last - 1
                act_hi(F0 + FT - 3, 1, 1, None)
                ahead(n)
                silu(s, F0 + FT - 2, 0)
                act_hi(F0 + FT - 2, 0, 2, None)
                ahead(n + 1)
                silu(s, F0 + FT - 1, 1)
                act_hi(F0 + FT - 1, 1, 3, None)
                ahead(n + 2)
                post_norm(s)

            unit = [0]

            def tick(s, count=1):
                u0, units = UNITS[s]
                for i in range(unit[0], unit[0] + count):
                    if 2 <= i < len(units) + 2:
                        kind, h, t = units[i - 2]
                        u = u0 + i - 2
                        n = 512 if kind == "dil" else SEQ
                        act.wait_ge(pT_done, u + 1)
                        if i >= 4:
                            act.wait_ge(o_done, u - 1)
                        act.activation(probT[:, i % 2, 0:n], ps[:, PT_BANK, 0:n],
                                       ACT.Copy).then_inc(pT_ready, 1)
                    if i < len(units):
                        kind, h, t = units[i]
                        u = u0 + i
                        n = 512 if kind == "dil" else SEQ
                        act.wait_ge(max_done, u + 1)
                        if i >= 2:
                            act.wait_ge(pT_done, u - 1)
                        src = sbias[:, i % 2, :] if kind == "dil" else ps[:, S_BANK + i % 2, 0:SEQ]
                        act.activation(prob[:, i % 2, 0:n], src, ACT.Exp, bias=neg_max[:, u:u + 1],
                                       accum_out=den[:, u:u + 1]).then_inc(p_done, 1)
                unit[0] += count

            def beside(s, n, ticks):
                ahead(n, 0)
                tick(s, ticks[0])
                ahead(n, 1)
                tick(s, sum(ticks[1:]))

            def out_hi(s, g):
                k = g + 1 + (4 if s == 4 else 0)
                dst = (h_hi if s == 1 else m_hi)[:, 2 * g:2 * g + 2, :].rearrange("p a b -> p (a b)")
                act.wait_ge(oT_done, k)
                act.activation(dst, ps[:, PT_BANK, :], ACT.Copy).then_inc(oh_hi, 1)

            def out_his(s, n0, ticks):
                for g in range(len(ticks) - 1):
                    beside(s, n0 + g, ticks[g][:3])
                    out_hi(s, g + 1)
                    tick(s, ticks[g][3])

            def mem_keys(s):
                act.wait_ge(w_used, BASES[s] + 1)
                act.activation(kmT[:, :, :].rearrange("p a b -> p (a b)"), ps[:, Y_BANK[s - 1], :],
                               ACT.Copy).then_inc(km_ready, 1)

            def mixer0():
                s, base = 1, BASES[1]
                for j in range(1, 5):
                    ahead(base + j)
                act.wait_ge(w_used, base + 5)
                for t in range(NT):
                    mean_square(("cq", 1, t), ps[:, 2 + t, 0:QL], float(QL) ** -0.5)
                    mean_square(("ckv", 1, t), ps[:, t, 0:KVL], float(KVL) ** -0.5)
                ahead(base + 5)
                act.wait_ge(w_used, base + 6)
                act.activation(qmT[:, :, :].rearrange("p a b -> p (a b)"), ps[:, 4, :], ACT.Copy,
                               scale=HD ** -0.5).then_inc(qm_ready, 1)
                act.wait_ge(latT_done, 1)
                for c in range(5):
                    g = gcol[:, (G_Q + c):(G_Q + c + 1)]
                    act.activation(m_hi[:, c, :], ps[:, 5 + c // 2, c % 2 * SEQ:(c % 2 + 1) * SEQ], ACT.Copy,
                                   scale=g).then_inc(lat_hi, 1)

                def take(c):
                    is_q, half, t = chunk(c)
                    act.wait_ge(*up_of(c))
                    if c >= 4:
                        act.wait_ge(tokT_done, c - 3)
                    w, own = (3 * QK, QK) if is_q else (3 * 2 * HD, NOPE)
                    src = ps[:, 2 * t:2 * t + 2, 0:w].rearrange("p b (h n) -> p b h n", h=3)
                    act.activation(tok[:, c % 4, :, 0:own].rearrange("p (b h) n -> p b h n", b=2),
                                   src[:, :, :, 0:own], ACT.Copy).then_inc(tok_a, 1)

                def turned(c):
                    is_q, half, t = chunk(c)
                    act.wait_ge(tokT_done, c + 1)
                    dst = (qT if is_q else kT)[0:QK, 6 * half:6 * half + 6, t * P:(t + 1) * P]
                    act.activation(dst.rearrange("p (b h) n -> p b h n", b=2),
                                   ps[0:QK, 2 * t:2 * t + 2, 0:3 * P].rearrange("p b (h n) -> p b h n", h=3),
                                   ACT.Copy, scale=QK ** -0.5 if is_q else 1.0).then_inc(tokT_a, 1)

                tick(s)
                for piece, ticks in enumerate(TICKS0):
                    beside(s, base + 6 + piece, ticks[:2])
                    take(2 * piece)
                    tick(s, ticks[2])
                    take(2 * piece + 1)
                    tick(s, ticks[3])
                    turned(2 * piece)
                    tick(s, ticks[4])
                    if piece == 3:
                        out_hi(s, 0)
                    tick(s, ticks[5])
                mem_gain(1)
                out_his(s, base + 10, TICKS0_OUT)
                post_norm(s)

            def mixer1():
                s, base = 4, BASES[4]
                ahead(base)
                act.wait_ge(w_used, base + 1)
                act.activation(qmT[:, :, :].rearrange("p a b -> p (a b)"), ps[:, 0, :], ACT.Copy,
                               scale=HD ** -0.5).then_inc(qm_ready, 1)
                for j, (kind, g, p) in enumerate(STEPS1):
                    n, b = base + 1 + j, (1 + j) % 4
                    if j < len(STEPS1) - 1:
                        beside(s, n, TICKS1[j])
                    else:
                        beside(s, n, TICKS1[j][:3])
                        out_hi(s, 0)
                        tick(s, TICKS1[j][3])
                    if j % 2 == 0:
                        act.wait_ge(w_used, n + 1)
                        if kind == "qk":
                            act.activation(q1T[:, g, p, :], ps[:, b, 0:SEQ], ACT.Copy,
                                           scale=HD ** -0.5).then_inc(z1_a, 1)
                            act.activation(k1T[:, g, p, :], ps[:, b, SEQ:2 * SEQ], ACT.Copy).then_inc(z1_a, 1)
                        else:
                            dst, src = value_rows(kind, p, b)
                            act.activation(dst, src, ACT.Copy).then_inc(z1_a, 1)
                out_his(s, base + 19, TICKS1_OUT)
                post_norm(s)

            for t in range(NT):
                mean_square_x(0, t)
            for n in range(LOOKAHEAD):
                split(n, n, 1)
            for s in range(6):
                if FILLERS[s] and s != 3:
                    ahead(BASES[s])
                    mem_keys(s)
                elif s == 3:
                    ahead(BASES[s])
                pre_norm(s)
                unit[0] = 0
                if s == 1:
                    mixer0()
                elif s == 4:
                    mixer1()
                else:
                    ffn(s)

        @block.vector
        def _(dve):
            def split(n, slot, half=None):
                dve.wait_ge(hi_ready, 2 * n + (1 if half == 0 else 2))
                c = slice(0, PIECE) if half is None else slice(half * PIECE // 2, (half + 1) * PIECE // 2)
                dve.tensor_tensor(w_lo[:, slot, c], raw[:, slot, c], w_hi[:, slot, c].bitcast(F32),
                                  ALU.subtract).then_inc(lo_ready, 2 if half is None else 1)

            def ahead(n, half=None):
                n += LOOKAHEAD
                if n < PIECES:
                    split(n, n % RING, half)

            def normalise(s, t):
                r, ready = root_of(("x", s, t))
                dve.wait_ge(rstd_ready, ready)
                dve.tensor_scalar(work[:, t, :], x[:, t, :], r, None, ALU.mult).then_inc(xn_ready, 1)

            def pre_norm(s):
                if s == 0:
                    dve.wait_ge(gcol_in, 16)
                for kt in range(KT):
                    dve.wait_ge(h_hi_ready, KT * s + kt // 2 * 2 + 2)
                    dve.scalar_tensor_tensor(h_lo[:, kt, :],
                                             ps[:, X_BANK[s] + kt // 2, kt % 2 * SEQ:(kt % 2 + 1) * SEQ],
                                             gain(s // 3, 2 * (s % 3), kt), h_hi[:, kt, :].bitcast(F32),
                                             ALU.mult, ALU.subtract).then_inc(h_lo_ready, 1)

            def post_norm(s):
                last = BASES[s] + COUNTS[s] - 1
                for t in range(NT):
                    r, ready = root_of(("y", s, t))
                    b = Y_BANK[s] + 2 * t
                    dve.wait_ge(ms_ready, ready)
                    dve.wait_ge(g_row_in, 16 * (s + 1))
                    dve.tensor_tensor(work[:, t, :].rearrange("p (b n) -> p b n", b=2), ps[:, b:b + 2, :],
                                      g_row[:, :].rearrange("p (b n) -> p b n", b=2),
                                      ALU.mult).then_inc(yg_done, 1)
                    dve.wait_ge(yg_done, NT * s + t + 1)
                    dve.wait_ge(rstd_ready, ready)
                    dve.scalar_tensor_tensor(x[:, t, :], work[:, t, :], r,
                                             x[:, t, :], ALU.mult, ALU.add).then_inc(x_ready, 1)
                    if s < 5:
                        if t == NT - 1:
                            ahead(last, 0)
                        normalise(s + 1, t)
                        if t == NT - 1:
                            ahead(last, 1)

            def act_mul(s, F, f, n):
                dve.wait_ge(silu_done, F + 1)
                dve.wait_ge(w_used, n + 1)
                if not isinstance(F, int) or F >= 2:
                    dve.wait_ge(a_hi_ready, F - 1)
                dve.tensor_tensor(act_f[:, f % 2, :], silu_g[:, f % 2, :], ps[:, GU_BANK[s] + 2 + f % 2, 0:SEQ],
                                  ALU.mult).then_inc(a_done, 1)

            def act_lo(F, f, slot):
                dve.wait_ge(a_hi_ready, F + 1)
                dve.tensor_tensor(a_lo[:, slot, :], act_f[:, f % 2, :], a_hi[:, slot, :].bitcast(F32),
                                  ALU.subtract).then_inc(a_lo_ready, 1)

            def mem_norm():
                for t in range(NT):
                    r, ready = root_of(("mem", 0, t))
                    dve.wait_ge(rstd_ready, ready)
                    dve.tensor_scalar(work[:, t, :], work[:, t, :], r, None,
                                      ALU.mult).then_inc(memn_ready, 1)

            def mem_gain(layer):
                for kt in range(KT):
                    dve.wait_ge(m_hi_ready, KT * layer + kt + 1)
                    dve.scalar_tensor_tensor(m_lo[:, kt, :], memT[:, kt, :], gain(layer, 6, kt),
                                             m_hi[:, kt, :].bitcast(F32), ALU.mult,
                                             ALU.subtract).then_inc(m_lo_ready, 1)

            def ffn(s):
                base, F0 = BASES[s] + FILLERS[s], FT * FFNS[s]
                ahead(base)
                act_mul(s, F0, 0, base)
                if s == 0:
                    mem_norm()
                act_lo(F0, 0, 0)
                ahead(base + 1)
                act_mul(s, F0 + 1, 1, base + 1)
                if s == 0:
                    mem_gain(0)

                def period(c):
                    n = base + 3 * c - 1
                    F = F0 + 2 * c
                    r = (base - 1 + LOOKAHEAD) % RING
                    act_lo(F - 1, 1, 1)
                    split(n + 2, r)
                    act_mul(s, F, 0, n)
                    split(n + 3, (r + 1) % RING)
                    act_lo(F, 0, 0)
                    split(n + 4, (r + 2) % RING)
                    act_mul(s, F + 1, 1, n + 2)

                period(1)
                last = FT // 2 - 1
                with dve.Fori(2, last) as c:
                    period(c)
                n = base + 3 * last - 1
                act_lo(F0 + FT - 3, 1, 1)
                ahead(n)
                act_mul(s, F0 + FT - 2, 0, n)
                act_lo(F0 + FT - 2, 0, 2)
                ahead(n + 1)
                act_mul(s, F0 + FT - 1, 1, n + 1)
                act_lo(F0 + FT - 1, 1, 3)
                ahead(n + 2)
                post_norm(s)

            def mem_values(s):
                n, b = (BASES[1] + 2, 1) if s == 1 else (BASES[3] + 1, Y_BANK[2])
                dve.wait_ge(w_used, n)
                dve.tensor_copy(vm[:, :, :].rearrange("p a b -> p (a b)"), ps[:, b, :]).then_inc(vm_ready, 1)

            unit = [0]

            def tick(s, count=1):
                u0, units = UNITS[s]
                for i in range(unit[0], unit[0] + count):
                    if i < len(units):
                        kind, h, t = units[i]
                        u = u0 + i
                        dve.wait_ge(s_done, u + 1)
                        src = ps[:, S_BANK + i % 2, 0:SEQ]
                        if kind == "dil":
                            if i >= 2:
                                dve.wait_ge(p_done, u - 1)
                            dve.scalar_tensor_tensor(sbias[:, i % 2, :], dist[:, t, :], -(ALIBI_STEP ** (h + 1)),
                                                     ps[:, S_BANK + i % 2, :], ALU.mult, ALU.add).then_inc(sb_done, 1)
                            dve.wait_ge(sb_done, i - 2 * MEM_HEADS + 1)
                            src = sbias[:, i % 2, :]
                        dve.tensor_reduce(neg_max[:, u:u + 1], src, AX_X, ALU.max,
                                          negate=True).then_inc(max_done, 1)
                    if 3 <= i < len(units) + 3:
                        kind, h, t = units[i - 3]
                        u = u0 + i - 3
                        c = o_cols(s, kind, h)
                        dve.wait_ge(o_done, u + 1)
                        dve.wait_ge(rden_done, u + 1)
                        dve.tensor_scalar(work[:, t, c:c + HD], ps[:, O_BANK, 0:HD], rden[:, u:u + 1], None,
                                          ALU.mult).then_inc(o_ready, 1)
                    if 2 <= i < len(units) + 2:
                        u = u0 + i - 2
                        dve.wait_ge(p_done, u + 1)
                        dve.reciprocal(rden[:, u:u + 1], den[:, u:u + 1]).then_inc(rden_done, 1)
                unit[0] += count

            def beside(s, n, ticks):
                tick(s, ticks[0])
                ahead(n, 0)
                tick(s, ticks[1])
                ahead(n, 1)
                tick(s, sum(ticks[2:]))

            def out_lo(s, g):
                k = g + 1 + (4 if s == 4 else 0)
                hi, lo = ((h_hi, h_lo) if s == 1 else (m_hi, m_lo))
                hi, lo = (w[:, 2 * g:2 * g + 2, :].rearrange("p a b -> p (a b)") for w in (hi, lo))
                dve.wait_ge(oh_hi, k)
                dve.tensor_tensor(lo, ps[:, PT_BANK, :], hi.bitcast(F32), ALU.subtract).then_inc(oh_lo, 1)

            def out_los(s, n0, ticks):
                for g in range(len(ticks) - 1):
                    beside(s, n0 + g, ticks[g][:3])
                    out_lo(s, g + 1)
                    tick(s, ticks[g][3])

            def rotate(dst, src, temp, cos, sin, done, temps):
                lo, hi = slice(0, 16), slice(16, 32)
                dve.tensor_tensor(temp[0], src, cos, ALU.mult).then_inc(temps, 1)
                dve.tensor_tensor(temp[1][:, :, lo], src[:, :, hi], sin[:, :, lo], ALU.mult).then_inc(temps, 1)
                dve.tensor_tensor(temp[1][:, :, hi], src[:, :, lo], sin[:, :, hi], ALU.mult).then_inc(temps, 1)
                rotated[0] += 3
                dve.wait_ge(temps, rotated[0])
                dve.tensor_tensor(dst, temp[0], temp[1], ALU.add).then_inc(done, 1)

            rotated = [0]

            def mixer0():
                s, base = 1, BASES[1]
                ahead(base + 1)
                mem_values(s)
                for j in range(2, 5):
                    ahead(base + j)
                for t in range(NT):
                    for kind, a, n, bank in (("cq", 0, QL, 2), ("ckv", QL, KVL, 0)):
                        r, ready = root_of((kind, 1, t))
                        dve.wait_ge(rstd_ready, ready)
                        dve.tensor_scalar(zc[:, t, a:a + n], ps[:, bank + t, 0:n], r, None,
                                          ALU.mult).then_inc(lat_ready, 1)
                dve.wait_ge(rope_ready, 2)
                t2 = [rt[:, i, 0:2 * ROPE].rearrange("p (t n) -> p t n", t=2) for i in range(2)]
                rotate(kr[:, :, :], ps[:, 2:4, QL:QL + ROPE], t2, cc[:, :, :], ss[:, :, :], kr_ready, rope_tmp)
                ahead(base + 5)
                for c in range(5):
                    dve.wait_ge(lat_hi, min(c // 2 * 2 + 2, 5))
                    dve.scalar_tensor_tensor(m_lo[:, c, :], ps[:, 5 + c // 2, c % 2 * SEQ:(c % 2 + 1) * SEQ],
                                             gcol[:, G_Q + c:G_Q + c + 1], m_hi[:, c, :].bitcast(F32), ALU.mult,
                                             ALU.subtract).then_inc(lat_lo, 1)

                def take(c):
                    is_q, half, t = chunk(c)
                    dve.wait_ge(tok_a, c + 1)
                    if is_q:
                        dve.wait_ge(tok_d, c) if c else dve.wait_ge(kr_ready, 1)
                        shape = [P, 6, ROPE]
                        rotate(tok[:, c % 4, :, NOPE:QK], tok[:, c % 4, :, NOPE:QK],
                               [rt[:, i, :].rearrange("p (h n) -> p h n", h=6) for i in range(2)],
                               cc[:, t:t + 1, :].broadcast_to(shape), ss[:, t:t + 1, :].broadcast_to(shape),
                               tok_d, rope_tmp)
                    else:
                        src = ps[:, 2 * t:2 * t + 2, 0:3 * 2 * HD].rearrange("p b (h n) -> p b h n", h=3)
                        dve.tensor_copy(v0[:, t, 6 * half:6 * half + 6, :].rearrange("p (b h) n -> p b h n", b=2),
                                        src[:, :, :, HD:2 * HD]).then_inc(tok_d, 1)

                def turned(c):
                    is_q, half, t = chunk(c)
                    dve.wait_ge(tokT_done, c + 1)
                    dst = (qT if is_q else kT)[0:QK, 6 * half:6 * half + 6, t * P:(t + 1) * P]
                    dve.tensor_scalar(dst.rearrange("p (b h) n -> p b h n", b=2),
                                      ps[0:QK, 2 * t:2 * t + 2, 0:3 * P].rearrange("p b (h n) -> p b h n", h=3),
                                      QK ** -0.5 if is_q else 1.0, None, ALU.mult).then_inc(tokT_d, 1)

                tick(s)
                for piece, ticks in enumerate(TICKS0):
                    beside(s, base + 6 + piece, ticks[:2])
                    take(2 * piece)
                    tick(s, ticks[2])
                    take(2 * piece + 1)
                    tick(s, ticks[3] + ticks[4])
                    turned(2 * piece + 1)
                    if piece == 3:
                        out_lo(s, 0)
                    tick(s, ticks[5])
                mem_gain(1)
                out_los(s, base + 10, TICKS0_OUT)
                post_norm(s)

            def mixer1():
                s, base = 4, BASES[4]
                ahead(base)
                for j, (kind, g, p) in enumerate(STEPS1):
                    n, b = base + 1 + j, (1 + j) % 4
                    if j < len(STEPS1) - 1:
                        beside(s, n, TICKS1[j])
                    else:
                        beside(s, n, TICKS1[j][:3])
                        out_lo(s, 0)
                        tick(s, TICKS1[j][3])
                    if j % 2 == 1:
                        dve.wait_ge(w_used, n + 1)
                        if kind == "qk":
                            dve.tensor_scalar(q1T[:, g, p, :], ps[:, b, 0:SEQ], HD ** -0.5, None,
                                              ALU.mult).then_inc(z1_d, 1)
                            dve.tensor_copy(k1T[:, g, p, :], ps[:, b, SEQ:2 * SEQ]).then_inc(z1_d, 1)
                        else:
                            dst, src = value_rows(kind, p, b)
                            dve.tensor_copy(dst, src).then_inc(z1_d, 1)
                out_los(s, base + 19, TICKS1_OUT)
                post_norm(s)

            for t in range(NT):
                normalise(0, t)
            for n in range(LOOKAHEAD):
                split(n, n)
            for s in range(6):
                if FILLERS[s]:
                    ahead(BASES[s])
                    if s == 3:
                        mem_values(s)
                pre_norm(s)
                unit[0] = 0
                if s == 1:
                    mixer0()
                elif s == 4:
                    mixer1()
                else:
                    ffn(s)

        @block.tensor
        def _(pe):
            def arrived(n):
                pe.wait_ge(lo_ready, 2 * n + 2)

            def triple(out_ap, st_hi, st_lo, mv_hi, mv_lo, start, stop):
                pe.matmul(out_ap, st_hi, mv_hi, start=start, stop=False)
                pe.matmul(out_ap, st_hi, mv_lo, start=False, stop=False)
                return pe.matmul(out_ap, st_lo, mv_hi, start=False, stop=stop)

            def weights(slot):
                return (w[:, slot, :].rearrange("p (k n) -> p k n", k=KT) for w in (w_hi, w_lo))

            def pre_norm(s):
                if s == 0:
                    pe.wait_ge(ident_in, 16)
                for t in range(NT):
                    pe.wait_ge(xn_ready, NT * s + t + 1)
                    for kt in range(KT):
                        c = kt % 2 * SEQ + t * P
                        last = pe.transpose(ps[:, X_BANK[s] + kt // 2, c:c + P],
                                            work[:, t, kt * P:(kt + 1) * P], ident)
                    last.then_inc(xT_done, 1)

            def gate_up(s, F, f, n, slot, first=False):
                arrived(n)
                if not isinstance(F, int) or F >= 2:
                    pe.wait_ge(a_done, F - 1)
                for half in range(2):
                    wh, wl = (w[:, slot, half * 1024:(half + 1) * 1024].rearrange("p (k n) -> p k n", k=KT)
                              for w in (w_hi, w_lo))
                    for kt in range(KT):
                        if first and half == 0:
                            pe.wait_ge(h_lo_ready, KT * s + kt + 1)
                        last = triple(ps[:, GU_BANK[s] + 2 * half + f % 2, 0:SEQ], wh[:, kt, :], wl[:, kt, :],
                                      h_hi[:, kt, :], h_lo[:, kt, :], kt == 0, kt == KT - 1)
                    last.then_inc((g_done, w_used)[half], 1)

            def quarter(s, slot, src_hi, src_lo, row, j, t, first, last):
                sh, sl = src_hi[:, row, t * P:(t + 1) * P], src_lo[:, row, t * P:(t + 1) * P]
                for k, (st, w) in enumerate(((sh, w_hi), (sh, w_lo), (sl, w_hi))):
                    for half in range(2):
                        c = j * 1024 + half * 512
                        ins = pe.matmul(ps[:, Y_BANK[s] + 2 * t + half, :], st, w[:, slot, c:c + 512],
                                        start=first and k == 0, stop=last and k == 2)
                return ins

            def mem_transposes():
                pe.wait_ge(memn_ready, NT)
                for kt in range(KT):
                    for t in range(NT):
                        c = kt % 2 * NMEM + t * P
                        last = pe.transpose(ps[:, kt // 2, c:c + P], work[:, t, kt * P:(kt + 1) * P], ident)
                last.then_inc(memT_done, 1)

            def ffn(s):
                base, F0 = BASES[s] + FILLERS[s], FT * FFNS[s]
                gate_up(s, F0, 0, base, base % RING, first=True)
                if s == 0:
                    mem_transposes()
                if s == 2:
                    pe.wait_ge(km_ready, 2)
                if s == 3:
                    pe.wait_ge(vm_ready, 2)
                gate_up(s, F0 + 1, 1, base + 1, (base + 1) % RING)

                def period(c, first=False):
                    n = base + 3 * c - 1
                    F = F0 + 2 * c
                    r = (base - 1) % RING
                    gate_up(s, F, 0, n, r)
                    if first and s == 0:
                        pe.wait_ge(memT_ready, KT // 2)
                    arrived(n + 1)
                    pe.wait_ge(a_lo_ready, F)
                    for j in range(2):
                        for t in range(NT):
                            last = quarter(s, (r + 1) % RING, a_hi, a_lo, j, j, t, first and j == 0, False)
                    last.then_inc(w_used, 1)
                    gate_up(s, F + 1, 1, n + 2, (r + 2) % RING)

                period(1, first=True)
                last = FT // 2 - 1
                with pe.Fori(2, last) as c:
                    period(c)
                n = base + 3 * last - 1
                gate_up(s, F0 + FT - 2, 0, n, n % RING)
                gate_up(s, F0 + FT - 1, 1, n + 1, (n + 1) % RING)
                for t in range(NT):
                    for piece in range(2):
                        if t == 0:
                            arrived(n + 2 + piece)
                            pe.wait_ge(a_lo_ready, F0 + FT - 2 + 2 * piece)
                        for j in range(2):
                            ins = quarter(s, (n + 2 + piece) % RING, a_hi, a_lo, 2 * piece + j, j, t, False,
                                          piece == j == 1)
                        if t == NT - 1:
                            ins.then_inc(w_used, 1)
                    if t == 0:
                        ins.then_inc(y_done, 1)

            def columns(slot, out_ap, src_hi, src_lo):
                wh, wl = weights(slot)
                for m in range(2):
                    for kt in range(KT):
                        last = triple(out_ap[:, m * SEQ:(m + 1) * SEQ], wh[:, kt, m * P:(m + 1) * P],
                                      wl[:, kt, m * P:(m + 1) * P], src_hi[:, kt, :], src_lo[:, kt, :],
                                      kt == 0, kt == KT - 1)
                        if kt == KT // 2 - 1:
                            yield
                    if m == 1:
                        last.then_inc(w_used, 1)
                    yield

            def rows(slot, outs, width, src_hi, src_lo):
                wh, wl = weights(slot)
                for t in range(NT):
                    for kt in range(KT):
                        last = triple(outs[t], src_hi[:, kt, t * P:(t + 1) * P], src_lo[:, kt, t * P:(t + 1) * P],
                                      wh[:, kt, 0:width], wl[:, kt, 0:width], kt == 0, kt == KT - 1)
                        if kt == KT // 2 - 1:
                            yield
                    if t == NT - 1:
                        last.then_inc(w_used, 1)
                    yield

            def run(product):
                for _ in product:
                    pass

            def memory_keys(s):
                arrived(BASES[s])
                pe.wait_ge(m_lo_ready, KT * (2 if s > 1 else 1))
                pe.wait_ge(yg_done, NT * (s - 1) + 1)
                run(columns(BASES[s] % RING, ps[:, Y_BANK[s - 1], :], m_hi, m_lo))

            def memory_values(s):
                n, b = (BASES[1] + 1, 1) if s == 1 else (BASES[3], Y_BANK[2])
                arrived(n)
                if s == 3:
                    pe.wait_ge(yg_done, NT * (s - 1) + 1)
                run(rows(n % RING, [ps[:, b, t * 256:(t + 1) * 256] for t in range(2)], 256, m_hi, m_lo))

            unit = [0]
            pt_free = [None]

            def tick(s, count=1):
                u0, units = UNITS[s]
                for i in range(unit[0], unit[0] + count):
                    if i < len(units):
                        kind, h, t = units[i]
                        tok_cols = slice(t * P, (t + 1) * P)
                        if i >= 2:
                            pe.wait_ge(p_done, u0 + i - 1)
                        bank = ps[:, S_BANK + i % 2, :]
                        if kind == "mla":
                            if h % (MLA_HEADS // 2) == t == 0:
                                for turned in (tokT_a, tokT_d):
                                    pe.wait_ge(turned, 2 * (h // (MLA_HEADS // 2)) + 2)
                            last = pe.matmul(bank[:, 0:SEQ], qT[0:QK, h, tok_cols], kT[0:QK, h, :],
                                             start=True, stop=True)
                        else:
                            pr = slice(h % 2 * HD, (h % 2 + 1) * HD)
                            if kind == "mem":
                                last = pe.matmul(bank[:, 0:SEQ], qmT[pr, h // 2, tok_cols], kmT[pr, h // 2, :],
                                                 start=True, stop=True)
                            else:
                                if h % 2 == t == 0:
                                    for k in range(3):
                                        pe.wait_ge(*evacuated(STEPS1.index(("qk", k, h // 2))))
                                pe.matmul(bank[:, 0:SEQ], q1T[pr, 0, h // 2, tok_cols], k1T[pr, 0, h // 2, :],
                                          start=True, stop=True)
                                for g in (1, 2):
                                    last = pe.matmul(bank[:, SEQ + (g - 1) * P:SEQ + g * P],
                                                     q1T[pr, g, h // 2, tok_cols], k1T[pr, g, h // 2, tok_cols],
                                                     start=True, stop=True)
                        last.then_inc(s_done, 1)
                    if 2 <= i < len(units) + 2:
                        kind, h, t = units[i - 2]
                        j = i - 2
                        pe.wait_ge(p_done, u0 + j + 1)
                        if pt_free[0]:
                            pe.wait_ge(*pt_free[0])
                        for c in range(4 if kind == "dil" else 2):
                            last = pe.transpose(ps[:, PT_BANK, c * P:(c + 1) * P],
                                                prob[:, j % 2, c * P:(c + 1) * P], ident)
                        last.then_inc(pT_done, 1)
                        pt_free[0] = (pT_ready, u0 + j + 1)
                    if 3 <= i < len(units) + 3:
                        kind, h, t = units[i - 3]
                        j = i - 3
                        pe.wait_ge(pT_ready, u0 + j + 1)
                        if u0 + j:
                            pe.wait_ge(o_ready, u0 + j)
                        hc = slice(h * HD, (h + 1) * HD)
                        if kind == "dil":
                            if h % 2 == t == 0:
                                pe.wait_ge(*evacuated(STEPS1.index(("v01", 0, h // 2))))
                                pe.wait_ge(*evacuated(STEPS1.index(("v2", 2, h // 4 * 2))))
                            vals = [v1[:, 0, 0, hc], v1[:, 0, 1, hc], v1[:, 1, t, hc], v1[:, 2, t, hc]]
                        elif kind == "mla":
                            vals = [v0[:, c, h, :] for c in range(2)]
                        else:
                            vals = [vm[:, c, hc] for c in range(2)]
                        for c, v in enumerate(vals):
                            last = pe.matmul(ps[:, O_BANK, 0:HD], probT[:, j % 2, c * P:(c + 1) * P], v,
                                             start=c == 0, stop=c == len(vals) - 1)
                        last.then_inc(o_done, 1)
                unit[0] += count

            def turn_out(s, g):
                k0, needed = out_groups(s)[g]
                pe.wait_ge(o_ready, UNITS[s][0] + needed)
                pe.wait_ge(*pt_free[0])
                for k in range(2):
                    for t in range(NT):
                        c = k * SEQ + t * P
                        last = pe.transpose(ps[:, PT_BANK, c:c + P],
                                            work[:, t, (k0 + k) * P:(k0 + k + 1) * P], ident)
                last.then_inc(oT_done, 1)
                pt_free[0] = (oh_lo, g + 1 + (4 if s == 4 else 0))

            def project(s, n0, ticks):
                groups = len(ticks)
                src_hi, src_lo = (h_hi, h_lo) if s == 1 else (m_hi, m_lo)
                for g in range(groups):
                    arrived(n0 + g)
                    pe.wait_ge(oh_lo, g + 1 + (4 if s == 4 else 0))
                    for q in range(4):
                        j, t = (q % 2, q // 2) if g == groups - 1 else (q // 2, q % 2)
                        last = quarter(s, (n0 + g) % RING, src_hi, src_lo, 2 * g + j, j, t,
                                       g == 0 and j == 0, g == groups - 1 and j == 1)
                        if g == groups - 1 and q == 1:
                            last.then_inc(y_done, 1)
                        if q == 3:
                            last.then_inc(w_used, 1)
                        tick(s, ticks[g][q])
                        if q == 2 and g < groups - 1:
                            turn_out(s, g + 1)

            def mixer0():
                s, base = 1, BASES[1]
                pe.wait_ge(h_lo_ready, KT * (s + 1))
                arrived(base + 2)
                run(rows((base + 2) % RING, [ps[:, 2 + t, 0:256] for t in range(NT)], 256, h_hi, h_lo))
                arrived(base + 3)
                run(rows((base + 3) % RING, [ps[:, 2 + t, 256:256 + P + ROPE] for t in range(NT)], P + ROPE,
                         h_hi, h_lo))
                arrived(base + 4)
                pe.wait_ge(km_ready, 1)
                pe.wait_ge(vm_ready, 1)
                run(rows((base + 4) % RING, [ps[:, t, 0:256] for t in range(NT)], 256, h_hi, h_lo))
                arrived(base + 5)
                run(columns((base + 5) % RING, ps[:, 4, :], h_hi, h_lo))
                for t in range(NT):
                    pe.wait_ge(lat_ready, 2 * t + 2)
                    for c in range(5):
                        last = pe.transpose(ps[:, 5 + c // 2, c % 2 * SEQ + t * P:c % 2 * SEQ + (t + 1) * P],
                                            zc[:, t, c * P:(c + 1) * P], ident)
                last.then_inc(latT_done, 1)
                pt_free[0] = (lat_lo, 5)
                pe.wait_ge(qm_ready, 1)
                pe.wait_ge(lat_lo, 5)
                tick(s)

                def turn(c):
                    is_q, half, t = chunk(c)
                    pe.wait_ge(tok_a, c + 1)
                    pe.wait_ge(tok_d, c + 1)
                    if not is_q:
                        pe.wait_ge(tok_p, 2 * half + t + 1)
                    for h in range(6):
                        last = pe.transpose(ps[0:QK, 2 * t + h // 3, h % 3 * P:(h % 3 + 1) * P],
                                            tok[:, c % 4, h, :], ident)
                    last.then_inc(tokT_done, 1)

                for piece in range(4):
                    n = base + 6 + piece
                    arrived(n)
                    kts, k0, width = (3, 0, 3 * QK) if piece % 2 == 0 else (2, 3, 3 * 2 * HD)
                    for t in range(NT):
                        c = 2 * piece + t
                        if c == 0:
                            pe.wait_ge(kr_ready, 1)
                        if c >= 2:
                            pe.wait_ge((tokT_a, tokT_d)[t], piece)
                        for b in range(2):
                            if t or b:
                                tick(s, TICKS0[piece][2 * t + b - 1])
                            for k in range(kts):
                                o = k * 2 * width + b * width
                                last = triple(ps[:, 2 * t + b, 0:width], m_hi[:, k0 + k, t * P:(t + 1) * P],
                                              m_lo[:, k0 + k, t * P:(t + 1) * P], w_hi[:, n % RING, o:o + width],
                                              w_lo[:, n % RING, o:o + width], k == 0, k == kts - 1)
                        last.then_inc((up_done, w_used)[t], 1)
                    tick(s, TICKS0[piece][3])
                    turn(2 * piece)
                    tick(s, TICKS0[piece][4])
                    turn(2 * piece + 1)
                    if piece == 3:
                        turn_out(s, 0)
                    tick(s, TICKS0[piece][5])
                project(s, base + 10, TICKS0_OUT)

            def mixer1():
                s, base = 4, BASES[4]
                pe.wait_ge(h_lo_ready, KT * (s + 1))
                arrived(base)
                run(columns(base % RING, ps[:, 0, :], h_hi, h_lo))
                for k, (kind, g, p) in enumerate(STEPS1):
                    n, b = base + 1 + k, (1 + k) % 4
                    arrived(n)
                    if k == 0:
                        pe.wait_ge(qm_ready, 2)
                        pe.wait_ge(vm_ready, 2)
                        pe.wait_ge(km_ready, 2)
                    if k >= 4:
                        pe.wait_ge(*evacuated(k - 4))
                    if kind == "qk":
                        product = columns(n % RING, ps[:, b, :], h_hi, h_lo)
                    else:
                        product = rows(n % RING, [ps[:, b, t * 256:(t + 1) * 256] for t in range(NT)], 256,
                                       h_hi, h_lo)
                    for q, _ in enumerate(product):
                        if q == 3 and k == len(STEPS1) - 1:
                            turn_out(s, 0)
                        tick(s, TICKS1[k][q])
                for k in range(14, 18):
                    pe.wait_ge(*evacuated(k))
                project(s, base + 19, TICKS1_OUT)

            for s in range(6):
                unit[0] = 0
                if s in (1, 2):
                    memory_keys(s)
                if s == 3:
                    memory_values(s)
                pre_norm(s)
                if s == 1:
                    memory_values(s)
                    mixer0()
                elif s == 4:
                    mixer1()
                else:
                    ffn(s)


ROPE_STEPS = 1 + NT + 5 + 12 + 1 + 4


def _token_order():
    return np.arange(SEQ).reshape(SEQ // CLASSES, CLASSES).T.reshape(-1)


def _constants():
    token = _token_order()
    diff = np.abs(token[:, None] - token[None, :])
    table = []
    for g, (window, dil) in enumerate(GROUPS):
        seen = (diff % dil == 0) & (diff // dil <= window // (2 * dil))
        d = np.where(seen, diff * ALIBI_STEP ** (8 * g), MASKED)
        table.append(d)
    rows = []
    for t in range(NT):
        own = slice(t * P, (t + 1) * P)
        assert all((table[g][own, :P * NT].min(1) < MASKED).all() for g in range(3))
        rows.append(np.concatenate([table[0][own, :], table[1][own, own], table[2][own, own]], axis=1))
    dist = np.stack(rows, 1).reshape(P, -1)
    inv = np.float32(10000.0) ** (-np.arange(16, dtype=np.float32) / np.float32(16))
    return np.concatenate([np.eye(P), dist, np.broadcast_to(inv, (P, 16))], axis=1).astype(np.float32)


def _by_columns(w, cols):
    w = w[:, cols]
    k = w.shape[0] // P
    w = w.reshape(k, P, w.shape[1]).transpose(1, 0, 2)
    if k == KT and w.shape[2] < PIECE // KT:
        w = np.concatenate([w, np.zeros((P, k, PIECE // KT - w.shape[2]), w.dtype)], axis=2)
    w = w.reshape(P, -1)
    return np.concatenate([w, np.zeros((P, PIECE - w.shape[1]), w.dtype)], axis=1)


def _by_rows(w, kt):
    return w[kt * P:(kt + 2) * P].reshape(2, P, D).transpose(1, 0, 2).reshape(P, PIECE)


def _stream(a):
    pieces = []

    def ffn(l, i):
        wg, wu, wd = a["ffn_w_gate"][l, i], a["ffn_w_up"][l, i], a["ffn_w_down"][l, i]

        def gate_up(f):
            cols = slice(f * P, (f + 1) * P)
            pieces.append(np.concatenate(
                [w[:, cols].reshape(KT, P, P).transpose(1, 0, 2).reshape(P, -1) for w in (wg, wu)], axis=1))

        gate_up(0)
        gate_up(1)
        for c in range(1, FT // 2 - 1):
            gate_up(2 * c)
            pieces.append(_by_rows(wd, 2 * c - 2))
            gate_up(2 * c + 1)
        gate_up(FT - 2)
        gate_up(FT - 1)
        pieces.append(_by_rows(wd, FT - 4))
        pieces.append(_by_rows(wd, FT - 2))

    def memory(l, c):
        pieces.append(_by_columns(a["mem_w_kv"][l], slice(c * 256, (c + 1) * 256)))

    def out(w):
        n = w.shape[0] // P - 2
        for kt in (n, *range(0, n, 2)):
            pieces.append(_by_rows(w, kt))

    ffn(0, 0)
    memory(0, 0)
    memory(0, 1)
    w = a["a_w_in"][0]
    o2, o3 = QL + KVL, QL + KVL + ROPE
    pieces.append(_by_columns(w, slice(0, 256)))
    pieces.append(_by_columns(w, np.r_[256:QL, o2:o3]))
    pieces.append(_by_columns(w, slice(QL, o2)))
    pieces.append(_by_columns(w, slice(o3, o3 + 256)))
    for half in range(2):
        for w, n in ((a["a_w_uq"][0], QK), (a["a_w_ukv"][0], 2 * HD)):
            pieces.append(_by_columns(w, slice(half * 6 * n, (half + 1) * 6 * n)))
    out(a["a_w_out"][0])
    memory(1, 0)
    ffn(0, 1)
    memory(1, 1)
    ffn(1, 0)
    w = a["b_w_in"][0]
    width = DIL_HEADS * HD
    own = 3 * 3 * width
    pieces.append(_by_columns(w, slice(own, own + MEM_HEADS * HD)))

    def cols(g, which, p, pairs=1):
        c = (3 * g + which) * width + p * P
        return np.arange(c, c + pairs * P)

    for kind, g, p in STEPS1:
        if kind == "qk":
            c = np.concatenate([cols(g, 0, p), cols(g, 1, p)])
        elif kind == "v01":
            c = np.concatenate([cols(0, 2, p), cols(1, 2, p)])
        else:
            c = cols(2, 2, p, 2)
        pieces.append(_by_columns(w, c))
    out(a["b_w_out"][0])
    ffn(1, 1)
    assert len(pieces) == PIECES
    return np.stack(pieces)


def kernel(**inputs):
    from concourse import bacc
    from concourse.bass_utils import run_bass_kernel_spmd

    a = {k: np.asarray(v) for k, v in inputs.items()}
    order = _token_order()
    norm_g = a["norm_g"]
    arrays = {
        "x_in": a["x"][0][order].reshape(NT, P, D),
        "mem_in": a["mem"][0].reshape(NT, P, D),
        "pos_in": a["positions"][0][order].reshape(NT, P).T,
        "stream": _stream(a),
        "gcols": np.concatenate([norm_g.reshape(2 * 7 * KT, P).T, a["a_q_norm"].reshape(-1, P).T,
                                 a["a_kv_norm"].reshape(-1, P).T], axis=1),
        "grows": norm_g[:, [1, 3, 5]].reshape(6, D),
        "consts": _constants(),
    }
    arrays = {k: np.ascontiguousarray(v) for k, v in arrays.items()}
    nc = bacc.Bacc("TRN2", target_bir_lowering=False, num_devices=1)
    args = [nc.dram_tensor(k, v.shape, mybir.dt.from_np(v.dtype), kind="ExternalInput").ap()
            for k, v in arrays.items()]
    args.append(nc.dram_tensor("out", (NT, P, D), F32, kind="ExternalOutput").ap())
    build(nc, *args)
    r = run_bass_kernel_spmd(nc, [arrays], core_ids=[0])
    got = r.results[0]["out"].reshape(SEQ, D)
    back = np.argsort(order)
    return got[back].reshape(1, SEQ, D)
```

```python
from contextlib import ExitStack

import numpy as np
import concourse.bass as bass
from concourse import mybir

F32 = mybir.dt.float32
F32R = mybir.dt.float32r
I32 = mybir.dt.int32
ALU = mybir.AluOpType
ACT = mybir.ActivationFunctionType
AX_X = mybir.AxisListType.X

P = 128
D = 1024
KT = D // P
SEQ = 256
NT = SEQ // P
NMEM = 256
DFF = 2816
FT = DFF // P
EPS = 1e-6
HD = 64
MEM_HEADS = 4
MLA_HEADS = 12
NOPE, ROPE = 64, 32
QK = NOPE + ROPE
QL, KVL = 384, 256
DIL_HEADS = 8
GROUPS = ((128, 1), (512, 4), (2048, 16))
CLASSES = 4
ALIBI_STEP = 2.0 ** (-8.0 / 24)
MASKED = 1e30

PIECE = 2048
RING = 3
LOOKAHEAD = 2
FFN_PIECES = FT + FT // 2
MIX0_PIECES = 2 + 4 + 2 + 2 + 4
MIX1_PIECES = 1 + 18 + 3
FILLERS = (0, 2, 1, 1, 0, 0)
COUNTS = (FFN_PIECES, MIX0_PIECES, FFN_PIECES + 1, FFN_PIECES + 1, MIX1_PIECES, FFN_PIECES)
BASES = tuple(sum(COUNTS[:s]) for s in range(len(COUNTS)))
PIECES = sum(COUNTS)
FFNS = {0: 0, 2: 1, 3: 2, 5: 3}
Y_BANK = (0, 0, 4, 0, 0, 4)
X_BANK = (0, 4, 4, 0, 4, 4)
GU_BANK = {0: 4, 2: 0, 3: 4, 5: 0}
EARLY = (True, False, True, True, True, True)
FILL_BANK = {1: 0, 2: 1, 3: 5}
S_BANK, PT_BANK, O_BANK = 4, 6, 7
HALF_PI = float(np.pi / 2)
TP1 = float(np.float32(6.28125))
TP2 = float(np.float32(np.float64(2 * np.pi - TP1) // 2.0 ** -21 * 2.0 ** -21))
TP3 = float(2 * np.pi - TP1 - TP2)
ROUND = float(1.5 * 2 ** 23)

STEPS1 = []
for _p in range(4):
    STEPS1 += [("qk", g, _p) for g in range(3)] + [("v01", 0, _p)] + ([("v2", 2, _p)] if _p % 2 == 0 else [])
TICKS1 = [(0, 0, 0, 1), (0, 1, 0, 1), (1, 0, 1, 0), (1, 0, 1, 0), (0, 1, 0, 0), (0, 1, 0, 0),
          (0, 1, 0, 0), (1, 0, 1, 0), (0, 0, 1, 0), (0, 1, 0, 0), (0, 1, 0, 0), (0, 1, 0, 0),
          (0, 0, 1, 0), (0, 1, 0, 0), (0, 1, 0, 0), (0, 1, 0, 0), (0, 0, 0, 0), (0, 1, 1, 1)]
TICKS1_OUT = [(1, 1, 1, 1), (0, 0, 0, 0)]
TICKS0 = [(1, 1, 1, 1, 1, 0), (1, 0, 1, 0, 1, 0), (1, 1, 1, 1, 1, 1), (2, 1, 1, 1, 1, 0)]
TICKS0_OUT = [(1, 1, 1, 2), (2, 1, 1, 1), (2, 2, 1, 0)]

IDLE = {0: ((4, 0), (4, 5), (4, 4)), 1: ((7, 0), (1, 4), (1, 0))}
for _s in range(2, len(COUNTS)):
    _before, _between = (0, 8) if FILLERS[_s] else (8, 12)
    IDLE[_s] = ((X_BANK[_s] + 3, _before), (Y_BANK[_s - 1], _between), (Y_BANK[_s - 1], 4))

FRONT, BACK = range(KT // 2), range(KT // 2, KT)

C_ID, C_DIST, C_INV = 0, P, P + 2 * 512
C_N = C_INV + 16
G_Q = 2 * 7 * KT
G_KV = G_Q + QL // P
G_N = G_KV + KVL // P


def build(nc, x_in, mem_in, pos_in, stream, gcols, grows, consts, out):
    with ExitStack() as ctx:
        def sb(name, shape, dt=F32):
            return ctx.enter_context(nc.sbuf_tensor(name, shape, dt))

        def sem(name):
            return ctx.enter_context(nc.semaphore(name))

        raw = sb("raw", [P, RING, PIECE])
        w_hi = sb("w_hi", [P, RING, PIECE], F32R)
        w_lo = sb("w_lo", [P, RING, PIECE], F32R)
        x = sb("x", [P, NT, D])
        work = sb("work", [P, NT, D])
        junk = sb("junk", [P, D])
        h_hi = sb("h_hi", [P, KT, SEQ], F32R)
        h_lo = sb("h_lo", [P, KT, SEQ], F32R)
        memT = sb("memT", [P, KT, NMEM])
        m_hi = sb("m_hi", [P, KT, NMEM], F32R)
        m_lo = sb("m_lo", [P, KT, NMEM], F32R)
        a_hi = sb("a_hi", [P, 4, SEQ], F32R)
        a_lo = sb("a_lo", [P, 4, SEQ], F32R)
        kmT = sb("kmT", [P, 2, NMEM])
        vm = sb("vm", [P, 2, MEM_HEADS * HD])
        qmT = sb("qmT", [P, 2, SEQ])
        g_row = sb("g_row", [P, D])
        cst = sb("cst", [P, C_N])
        gcol = sb("gcol", [P, G_N])
        posi = sb("posi", [P, NT], I32)
        posf = sb("posf", [P, NT])
        ang = sb("ang", [P, NT, 6, 16])
        cc = sb("cc", [P, NT, 32])
        ss = sb("ss", [P, NT, 32])
        kr = sb("kr", [P, NT, ROPE])
        rt = sb("rt", [P, 2, 6 * ROPE])
        stat_ms = sb("stat_ms", [P, 32, 2])
        stat_ve = sb("stat_ve", [P, 32])
        rstd = sb("rstd", [P, 32])
        neg_half = sb("neg_half", [P, 1])
        NU = 32 + 24
        neg_max = sb("neg_max", [P, NU])
        den = sb("den", [P, NU])
        rden = sb("rden", [P, NU])
        MIX = 3 * 3072 + 3 * 1024
        mix = sb("mix", [P, MIX])
        ps = ctx.enter_context(nc.psum_tensor("ps", [P, 8, 512], F32))

        def part(off, *shape):
            n = int(np.prod(shape))
            v = mix[:, off:off + n]
            names = "abcd"[:len(shape)]
            kw = {c: s for c, s in zip(names[1:], shape[1:])}
            return v.rearrange(f"p ({' '.join(names)}) -> p {' '.join(names)}", **kw) if len(shape) > 1 else v

        silu_g = part(0, 2, SEQ)
        act_f = part(512, 2, SEQ)
        tok = part(0, 4, 6, QK)
        v0 = part(2304, NT, MLA_HEADS, HD)
        qT = part(3840, MLA_HEADS, SEQ)
        kT = part(6912, MLA_HEADS, SEQ)
        zc = part(9984, NT, QL + KVL)
        q1T = part(0, 3, 4, SEQ)
        k1T = part(3072, 3, 4, SEQ)
        v1 = part(6144, 3, NT, DIL_HEADS * HD)
        sbias = part(9216, 2, 512)
        prob = part(10240, 2, 512)
        probT = part(11264, 2, 512)

        ident = cst[:, C_ID:C_ID + P]
        dist = cst[:, C_DIST:C_DIST + 1024].rearrange("p (t n) -> p t n", t=2)
        inv_freq = cst[:, C_INV:C_INV + 16]

        w_landed = [sem(f"w_landed{i}") for i in range(RING)]
        hi_ready, lo_ready = sem("hi_ready"), sem("lo_ready")
        w_used = sem("w_used")
        ident_in, consts_in, gcol_in, mem_in_s, pos_s = (sem(n) for n in (
            "ident_in", "consts_in", "gcol_in", "mem_landed", "pos_landed"))
        x_in_s = [sem(f"x_landed{t}") for t in range(NT)]
        g_row_in = sem("g_row_in")
        half_set, rope_step, rope_sin, rope_ready = (sem(n) for n in (
            "half_set", "rope_step", "rope_sin", "rope_ready"))
        ms_ready, ve_ready, rstd_ready = sem("ms_ready"), sem("ve_ready"), sem("rstd_ready")
        x_ready, xn_a, xn_d, xT_done, h_hi_ready, h_lo_ready = (sem(n) for n in (
            "x_ready", "xn_a", "xn_d", "xT_done", "h_hi_ready", "h_lo_ready"))
        y_done, yg_done = sem("y_done"), sem("yg_done")
        memn_ready, memT_done, memT_ready = sem("memn_ready"), sem("memT_done"), sem("memT_ready")
        m_hi_ready, m_lo_ready, km_ready, vm_ready, qm_ready = (sem(n) for n in (
            "m_hi_ready", "m_lo_ready", "km_ready", "vm_ready", "qm_ready"))
        g_done, silu_done, a_done, a_hi_ready, a_lo_ready = (sem(n) for n in (
            "g_done", "silu_done", "a_done", "a_hi_ready", "a_lo_ready"))
        lat_ready, latT_done, lat_hi, lat_lo = (sem(n) for n in ("lat_ready", "latT_done", "lat_hi", "lat_lo"))
        kr_ready, up_done, tok_a, tok_d, tok_p, rope_tmp = (sem(n) for n in (
            "kr_ready", "up_done", "tok_a", "tok_d", "tok_p", "rope_tmp"))
        tokT_done, tokT_a, tokT_d = sem("tokT_done"), sem("tokT_a"), sem("tokT_d")
        z1_a, z1_d = sem("z1_a"), sem("z1_d")
        s_done, sb_done, max_done, p_done, pT_done, pT_ready, rden_done, o_done, o_ready = (
            sem(n) for n in ("s_done", "sb_done", "max_done", "p_done", "pT_done", "pT_ready",
                             "rden_done", "o_done", "o_ready"))
        oT_done, oh_hi, oh_lo = sem("oT_done"), sem("oh_hi"), sem("oh_lo")
        out_done = sem("out_done")

        block = ctx.enter_context(nc.Block())

        def gain(layer, r, kt):
            c = (layer * 7 + r) * KT + kt
            return gcol[:, c:c + 1]

        UNITS0 = [("mem", h, t) for h in range(MEM_HEADS) for t in range(NT)] + \
                 [("mla", h, t) for h in range(MLA_HEADS) for t in range(NT)]
        UNITS1 = [("mem", h, t) for h in range(MEM_HEADS) for t in range(NT)] + \
                 [("dil", h, t) for h in range(DIL_HEADS) for t in range(NT)]
        UNITS = {1: (0, UNITS0), 4: (len(UNITS0), UNITS1)}
        OWN = {1: MLA_HEADS * HD, 4: DIL_HEADS * HD}

        SQUARES = []
        SQUARES += [(kind, 0, t) for kind in ("x", "mem") for t in range(NT)]
        for s in range(len(BASES)):
            SQUARES += [(c, s, t) for t in range(NT) for c in ("cq", "ckv")] if s == 1 else []
            for t in range(NT):
                SQUARES += [("y", s, t)] + ([("x", s + 1, t)] if s < 5 else [])

        def root_of(key):
            k = SQUARES.index(key)
            return rstd[:, k:k + 1], k + 1

        def parts_of(key):
            return 1 if key[0] in ("cq", "ckv") else 2

        def sums_before(k):
            return sum(parts_of(key) for key in SQUARES[:k])

        def turned_cols(s, t, kt):
            t0, count = (t, 1) if EARLY[s] else (0, NT)
            c = kt % 2 * SEQ
            return slice(t0 * P, (t + 1) * P), slice(c + t0 * P, c + (t + 1) * P), count

        def y_of(s, t, b):
            return (w_used, BASES[s] + COUNTS[s]) if t == b == 1 else (y_done, 3 * s + 2 * t + b + 1)

        def up_of(c):
            return (up_done, c // 2 + 1) if c % 2 == 0 else (w_used, BASES[1] + 7 + c // 2)

        def chunk(c):
            return c % 4 < 2, c // 4, c % 2

        def out_groups(s):
            n = OWN[s] // P
            return [(n, 2 * MEM_HEADS)] + [(k, 2 * MEM_HEADS + 4 * (k + 2)) for k in range(0, n, 2)]

        def value_rows(kind, p, b):
            if kind == "v01":
                return (v1[:, 0:2, :, p * P:(p + 1) * P].rearrange("p g t n -> p t g n"),
                        ps[:, b, :].rearrange("p (t g n) -> p t g n", t=NT, g=2))
            return v1[:, 2, :, p * P:(p + 2) * P], ps[:, b, :].rearrange("p (t n) -> p t n", t=NT)

        def evacuated(k):
            count = sum(2 if STEPS1[i][0] == "qk" else 1 for i in range(k % 2, k + 1, 2))
            return (z1_a, z1_d)[k % 2], count

        def o_cols(s, kind, h):
            return (OWN[s] if kind == "mem" else 0) + h * HD

        @block.sync
        def _(sp):
            for t in range(NT):
                sp.dma_start(x[:, t, :], x_in[t]).then_inc(x_in_s[t], 16)
            sp.dma_start(cst[:, 0:P], consts[:, 0:P]).then_inc(ident_in, 16)
            sp.dma_start(gcol[:, :], gcols).then_inc(gcol_in, 16)

            def load(i, slot, wait):
                if wait:
                    sp.wait_ge(lo_ready, 2 * i - 2 * (RING - 1))
                sp.dma_start(raw[:, slot, :], stream[i]).then_inc(w_landed[slot], 16)

            for i in range(RING):
                load(i, i, False)
            sp.dma_start(posi[:, :], pos_in).then_inc(pos_s, 16)
            sp.dma_start(cst[:, P:C_N], consts[:, P:C_N]).then_inc(consts_in, 16)
            sp.wait_ge(xT_done, NT * KT // 2)
            for t in range(NT):
                sp.dma_start(work[:, t, :], mem_in[t]).then_inc(mem_in_s, 16)
            for s, base in enumerate(BASES):
                a = base + 6
                start = RING if s == 0 else BASES[s - 1] + 6
                full = start + (a - start) // RING * RING
                with sp.Fori(start, full - RING + 1, RING) as i:
                    for j in range(RING):
                        load(i + j, (start + j) % RING, True)
                for i in range(full, a):
                    load(i, i % RING, True)
                if s > 0:
                    sp.wait_ge(yg_done, 2 * NT * s)
                sp.dma_start(g_row[:, :], grows[s:s + 1, :].broadcast_to([P, D])).then_inc(g_row_in, 16)
            start = BASES[-1] + 6
            full = start + (PIECES - start) // RING * RING
            with sp.Fori(start, full - RING + 1, RING) as i:
                for j in range(RING):
                    load(i + j, (start + j) % RING, True)
            for i in range(full, PIECES):
                load(i, i % RING, True)
            for t in range(NT):
                for b in range(2):
                    cols = slice(b * D // 2, (b + 1) * D // 2)
                    sp.wait_ge(x_ready, 2 * (NT * (len(BASES) - 1) + t) + b + 1)
                    sp.dma_start(out[t][:, cols], x[:, t, cols]).then_inc(out_done, 16)
            sp.wait_ge(out_done, 16 * NT * 2)

        @block.gpsimd
        def _(pool):
            pool.memset(neg_half[:, :], -0.5).then_inc(half_set, 1)
            pool.wait_ge(half_set, 1)
            steps = [0]

            def link(ins):
                steps[0] += 1
                ins.then_inc(rope_step, 1)
                pool.wait_ge(rope_step, steps[0])

            def rotary_angles():
                pool.wait_ge(pos_s, 16)
                pool.wait_ge(consts_in, 16)
                link(pool.tensor_copy(posf[:, :], posi[:, :]))
                A, K1, K0, T, B, C = (ang[:, :, i, :] for i in range(6))
                for t in range(NT):
                    link(pool.tensor_scalar(A[:, t, :], inv_freq, posf[:, t:t + 1], None, ALU.mult))
                link(pool.tensor_scalar(T, A, 1.0 / (2 * np.pi), ROUND, ALU.mult, ALU.add))
                link(pool.tensor_scalar(T, T, -ROUND, None, ALU.add))
                link(pool.tensor_scalar(K1, T, 1.0 / 4096, ROUND, ALU.mult, ALU.add))
                link(pool.tensor_scalar(K1, K1, -ROUND, 4096.0, ALU.add, ALU.mult))
                link(pool.tensor_tensor(K0, T, K1, ALU.subtract))
                for part_of in (TP1, TP2, TP3):
                    for K in (K1, K0):
                        link(pool.tensor_scalar(B, K, -part_of, None, ALU.mult))
                        link(pool.tensor_tensor(A, A, B, ALU.add))
                pi = float(np.float32(np.pi)) - 1e-6
                link(pool.tensor_scalar(A, A, pi, -pi, ALU.min, ALU.max))
                link(pool.tensor_scalar(B, A, 0.0, 2.0, ALU.is_ge, ALU.mult))
                link(pool.tensor_scalar(B, B, -1.0, None, ALU.add))
                link(pool.tensor_tensor(B, A, B, ALU.mult))
                link(pool.tensor_scalar(C, B, -1.0, HALF_PI, ALU.mult, ALU.add))
                assert steps[0] == ROPE_STEPS
                pool.wait_ge(rope_sin, 2)
                pool.tensor_copy(cc[:, :, 16:32], cc[:, :, 0:16]).then_inc(rope_ready, 1)
                pool.tensor_scalar(ss[:, :, 0:16], ss[:, :, 16:32], -1.0, None, ALU.mult).then_inc(rope_ready, 1)

            for k, (kind, s, t) in enumerate(SQUARES):
                eps = 4 * EPS if kind == "y" and s in FFNS else EPS
                pool.wait_ge(ms_ready, sums_before(k + 1))
                if parts_of((kind, s, t)) == 2:
                    pool.tensor_scalar(stat_ve[:, k:k + 1], stat_ms[:, k, 0:1], stat_ms[:, k, 1:2], eps,
                                       ALU.add, ALU.add).then_inc(ve_ready, 1)
                else:
                    pool.tensor_scalar(stat_ve[:, k:k + 1], stat_ms[:, k, 0:1], eps, None,
                                       ALU.add).then_inc(ve_ready, 1)
                pool.wait_ge(ve_ready, k + 1)
                pool.tensor_tensor(rstd[:, k:k + 1], stat_ve[:, k:k + 1], neg_half[:, 0:1],
                                   ALU.pow).then_inc(rstd_ready, 1)
                if (kind, t) == ("mem", NT - 1):
                    rotary_angles()
                if (kind, t) == ("ckv", NT - 1):
                    pool.wait_ge(kr_ready, 1)
                    for c in (2, 3, 6, 7):
                        if c >= 4:
                            pool.wait_ge(tokT_done, c - 3)
                        pool.tensor_copy(tok[:, c % 4, :, NOPE:QK],
                                         kr[:, c % 2:c % 2 + 1, :].broadcast_to([P, 6, ROPE])).then_inc(tok_p, 1)

        @block.scalar
        def _(act):
            def mean_square(key, src, scale, half=0):
                k = SQUARES.index(key)
                m = sums_before(k) + half
                if m >= 2:
                    act.wait_ge(ms_ready, m - 1)
                c = m % 2 * D // 2
                act.activation(junk[:, c:c + src.shape[-1]], src, ACT.Square, scale=scale,
                               accum_out=stat_ms[:, k, half:half + 1]).then_inc(ms_ready, 1)

            def normalise(s, t):
                r, ready = root_of(("x", s, t))
                act.wait_ge(rstd_ready, ready)
                act.activation(work[:, t, 0:D // 2], x[:, t, 0:D // 2], ACT.Copy, scale=r).then_inc(xn_a, 1)

            def split(n, slot, count, half=None):
                if half != 1:
                    act.wait_ge(w_landed[slot], 16 * count)
                    if not isinstance(n, int) or n >= RING:
                        act.wait_ge(w_used, n - (RING - 1))
                c = slice(0, PIECE) if half is None else slice(half * PIECE // 2, (half + 1) * PIECE // 2)
                act.activation(w_hi[:, slot, c], raw[:, slot, c],
                               ACT.Copy).then_inc(hi_ready, 2 if half is None else 1)

            def ahead(n, half=None):
                n += LOOKAHEAD
                if n < PIECES:
                    split(n, n % RING, n // RING + 1, half)

            def mean_square_x(s, t):
                for b in range(2):
                    if s == 0:
                        act.wait_ge(x_in_s[t], 16)
                    else:
                        act.wait_ge(x_ready, 2 * (NT * (s - 1) + t) + b + 1)
                    mean_square(("x", s, t), x[:, t, b * D // 2:(b + 1) * D // 2], 1.0 / 32, b)

            def pre_norm(s, t, kts=range(KT)):
                for kt in kts:
                    act.wait_ge(xT_done, KT // 2 * (NT * s + t) + kt // 2 + 1)
                    cols, c, count = turned_cols(s, t, kt)
                    act.activation(h_hi[:, kt, cols], ps[:, X_BANK[s] + kt // 2, c],
                                   ACT.Copy, scale=gain(s // 3, 2 * (s % 3), kt)).then_inc(h_hi_ready, count)

            def post_norm(s):
                last = BASES[s] + COUNTS[s] - 1
                for t in range(NT):
                    for b in range(2):
                        act.wait_ge(*y_of(s, t, b))
                        mean_square(("y", s, t), ps[:, Y_BANK[s] + 2 * t + b, :],
                                    (2.0 if s in FFNS else 1.0) / 32, b)
                    if s == 5:
                        continue
                    early = EARLY[s + 1]
                    if t == NT - 1:
                        normalise(s + 1, 0)
                        if not early or FILLERS[s + 1]:
                            ahead(last, 0)
                        if early:
                            pre_norm(s + 1, 0, FRONT)
                    mean_square_x(s + 1, t)
                    if t == NT - 1:
                        if early:
                            pre_norm(s + 1, 0, BACK)
                        else:
                            ahead(last, 1)
                        normalise(s + 1, t)
                        if early and FILLERS[s + 1]:
                            ahead(last, 1)

            def silu(s, F, f):
                act.wait_ge(g_done, F + 1)
                if not isinstance(F, int) or F >= 2:
                    act.wait_ge(a_done, F - 1)
                act.activation(silu_g[:, f % 2, :], ps[:, GU_BANK[s] + f % 2, 0:SEQ], ACT.Silu).then_inc(silu_done, 1)

            def act_hi(F, f, slot, used):
                act.wait_ge(a_done, F + 1)
                if used is not None:
                    act.wait_ge(w_used, used)
                act.activation(a_hi[:, slot, :], act_f[:, f % 2, :], ACT.Copy).then_inc(a_hi_ready, 1)

            def mem_squares():
                act.wait_ge(mem_in_s, 16 * NT)
                for t in range(NT):
                    for b in range(2):
                        mean_square(("mem", 0, t), work[:, t, b * D // 2:(b + 1) * D // 2], 1.0 / 32, b)

            def mem_turned():
                act.wait_ge(memT_done, 1)
                for b in range(KT // 2):
                    act.activation(memT[:, 2 * b:2 * b + 2, :].rearrange("p a b -> p (a b)"), ps[:, b, :],
                                   ACT.Copy).then_inc(memT_ready, 1)

            def mem_gain(layer):
                act.wait_ge(memT_ready, KT // 2)
                for kt in range(KT):
                    act.activation(m_hi[:, kt, :], memT[:, kt, :], ACT.Copy,
                                   scale=gain(layer, 6, kt)).then_inc(m_hi_ready, 1)

            def ffn(s):
                base, F0 = BASES[s] + FILLERS[s], FT * FFNS[s]
                ahead(base)
                silu(s, F0, 0)
                if s == 0:
                    mem_squares()
                act_hi(F0, 0, 0, None)
                ahead(base + 1)
                silu(s, F0 + 1, 1)
                if s == 0:
                    mem_turned()

                def period(c):
                    n = base + 3 * c - 1
                    F = F0 + 2 * c
                    r = (base - 1 + LOOKAHEAD) % RING
                    q = (base - 1 + LOOKAHEAD) // RING
                    act_hi(F - 1, 1, 1, None)
                    split(n + 2, r, c + q + 1)
                    silu(s, F, 0)
                    split(n + 3, (r + 1) % RING, c + q + 1 + (r + 1) // RING)
                    act_hi(F, 0, 0, n + 2)
                    split(n + 4, (r + 2) % RING, c + q + 1 + (r + 2) // RING)
                    silu(s, F + 1, 1)

                period(1)
                if s == 0:
                    mem_gain(0)
                    act.wait_ge(rope_step, ROPE_STEPS)
                    act.activation(ss[:, :, 16:32], ang[:, :, 0, :], ACT.Sin).then_inc(rope_sin, 1)
                    act.activation(cc[:, :, 0:16], ang[:, :, 5, :], ACT.Sin).then_inc(rope_sin, 1)
                last = FT // 2 - 1
                with act.Fori(2, last) as c:
                    period(c)
                n = base + 3 * last - 1
                act_hi(F0 + FT - 3, 1, 1, None)
                ahead(n)
                silu(s, F0 + FT - 2, 0)
                act_hi(F0 + FT - 2, 0, 2, None)
                ahead(n + 1)
                silu(s, F0 + FT - 1, 1)
                act_hi(F0 + FT - 1, 1, 3, None)
                ahead(n + 2)
                post_norm(s)

            unit = [0]

            def tick(s, count=1):
                u0, units = UNITS[s]
                for i in range(unit[0], unit[0] + count):
                    if 2 <= i < len(units) + 2:
                        kind, h, t = units[i - 2]
                        u = u0 + i - 2
                        n = 512 if kind == "dil" else SEQ
                        act.wait_ge(pT_done, u + 1)
                        if i >= 4:
                            act.wait_ge(o_done, u - 1)
                        act.activation(probT[:, i % 2, 0:n], ps[:, PT_BANK, 0:n],
                                       ACT.Copy).then_inc(pT_ready, 1)
                    if i < len(units):
                        kind, h, t = units[i]
                        u = u0 + i
                        n = 512 if kind == "dil" else SEQ
                        act.wait_ge(max_done, u + 1)
                        if i >= 2:
                            act.wait_ge(pT_done, u - 1)
                        src = sbias[:, i % 2, :] if kind == "dil" else ps[:, S_BANK + i % 2, 0:SEQ]
                        act.activation(prob[:, i % 2, 0:n], src, ACT.Exp, bias=neg_max[:, u:u + 1],
                                       accum_out=den[:, u:u + 1]).then_inc(p_done, 1)
                unit[0] += count

            def beside(s, n, ticks):
                ahead(n, 0)
                tick(s, ticks[0])
                ahead(n, 1)
                tick(s, sum(ticks[1:]))

            def out_hi(s, g):
                k = g + 1 + (4 if s == 4 else 0)
                dst = (h_hi if s == 1 else m_hi)[:, 2 * g:2 * g + 2, :].rearrange("p a b -> p (a b)")
                act.wait_ge(oT_done, k)
                act.activation(dst, ps[:, PT_BANK, :], ACT.Copy).then_inc(oh_hi, 1)

            def out_his(s, n0, ticks):
                for g in range(len(ticks)):
                    beside(s, n0 + g, ticks[g][:3])
                    out_hi(s, g + 1)
                    tick(s, ticks[g][3])

            def mem_keys(s):
                act.wait_ge(w_used, BASES[s] + 1)
                act.activation(kmT[:, :, :].rearrange("p a b -> p (a b)"), ps[:, FILL_BANK[s], :],
                               ACT.Copy).then_inc(km_ready, 1)

            def mixer0():
                s, base = 1, BASES[1]
                for j in range(1, 5):
                    ahead(base + j)
                act.wait_ge(w_used, base + 5)
                for t in range(NT):
                    mean_square(("cq", 1, t), ps[:, 2 + t, 0:QL], float(QL) ** -0.5)
                    mean_square(("ckv", 1, t), ps[:, t, 0:KVL], float(KVL) ** -0.5)
                act.wait_ge(latT_done, 1)
                for c in range(5):
                    g = gcol[:, (G_Q + c):(G_Q + c + 1)]
                    act.activation(m_hi[:, c, :], ps[:, 5 + c // 2, c % 2 * SEQ:(c % 2 + 1) * SEQ], ACT.Copy,
                                   scale=g).then_inc(lat_hi, 1)
                act.wait_ge(w_used, base + 6)
                act.activation(qmT[:, :, :].rearrange("p a b -> p (a b)"), ps[:, 4, :], ACT.Copy,
                               scale=HD ** -0.5).then_inc(qm_ready, 1)
                ahead(base + 5)

                def take(c):
                    is_q, half, t = chunk(c)
                    act.wait_ge(*up_of(c))
                    if c >= 4:
                        act.wait_ge(tokT_done, c - 3)
                    w, own = (3 * QK, QK) if is_q else (3 * 2 * HD, NOPE)
                    src = ps[:, 2 * t:2 * t + 2, 0:w].rearrange("p b (h n) -> p b h n", h=3)
                    act.activation(tok[:, c % 4, :, 0:own].rearrange("p (b h) n -> p b h n", b=2),
                                   src[:, :, :, 0:own], ACT.Copy).then_inc(tok_a, 1)

                def turned(c):
                    is_q, half, t = chunk(c)
                    act.wait_ge(tokT_done, c + 1)
                    dst = (qT if is_q else kT)[0:QK, 6 * half:6 * half + 6, t * P:(t + 1) * P]
                    act.activation(dst.rearrange("p (b h) n -> p b h n", b=2),
                                   ps[0:QK, 2 * t:2 * t + 2, 0:3 * P].rearrange("p b (h n) -> p b h n", h=3),
                                   ACT.Copy, scale=QK ** -0.5 if is_q else 1.0).then_inc(tokT_a, 1)

                for piece, ticks in enumerate(TICKS0):
                    beside(s, base + 6 + piece, ticks[:2])
                    take(2 * piece)
                    tick(s, ticks[2])
                    take(2 * piece + 1)
                    tick(s, ticks[3])
                    turned(2 * piece)
                    tick(s, ticks[4])
                    if piece == 3:
                        out_hi(s, 0)
                    tick(s, ticks[5])
                mem_gain(1)
                out_his(s, base + 10, TICKS0_OUT)
                post_norm(s)

            def mixer1():
                s, base = 4, BASES[4]
                ahead(base)
                act.wait_ge(w_used, base + 1)
                act.activation(qmT[:, :, :].rearrange("p a b -> p (a b)"), ps[:, 0, :], ACT.Copy,
                               scale=HD ** -0.5).then_inc(qm_ready, 1)
                for j, (kind, g, p) in enumerate(STEPS1):
                    n, b = base + 1 + j, (1 + j) % 4
                    if j < len(STEPS1) - 1:
                        beside(s, n, TICKS1[j])
                    else:
                        beside(s, n, TICKS1[j][:3])
                        out_hi(s, 0)
                        tick(s, TICKS1[j][3])
                    if j % 2 == 0:
                        act.wait_ge(w_used, n + 1)
                        if kind == "qk":
                            act.activation(q1T[:, g, p, :], ps[:, b, 0:SEQ], ACT.Copy,
                                           scale=HD ** -0.5).then_inc(z1_a, 1)
                            act.activation(k1T[:, g, p, :], ps[:, b, SEQ:2 * SEQ], ACT.Copy).then_inc(z1_a, 1)
                        else:
                            dst, src = value_rows(kind, p, b)
                            act.activation(dst, src, ACT.Copy).then_inc(z1_a, 1)
                out_his(s, base + 19, TICKS1_OUT)
                post_norm(s)

            for t in range(NT):
                mean_square_x(0, t)
                normalise(0, t)
            act.wait_ge(gcol_in, 16)
            pre_norm(0, 0)
            split(0, 0, 1, 0)
            for s in range(6):
                if s == 1:
                    ahead(BASES[s])
                    mem_keys(s)
                pre_norm(s, NT - 1)
                if s == 0:
                    split(0, 0, 1, 1)
                    split(1, 1, 1)
                elif FILLERS[s] == 1:
                    ahead(BASES[s])
                    if s == 2:
                        mem_keys(s)
                elif EARLY[s]:
                    ahead(BASES[s] - 1)
                unit[0] = 0
                if s == 1:
                    mixer0()
                elif s == 4:
                    mixer1()
                else:
                    ffn(s)

        @block.vector
        def _(dve):
            def split(n, slot, half=None):
                dve.wait_ge(hi_ready, 2 * n + (1 if half == 0 else 2))
                c = slice(0, PIECE) if half is None else slice(half * PIECE // 2, (half + 1) * PIECE // 2)
                dve.tensor_tensor(w_lo[:, slot, c], raw[:, slot, c], w_hi[:, slot, c].bitcast(F32),
                                  ALU.subtract).then_inc(lo_ready, 2 if half is None else 1)

            def ahead(n, half=None):
                n += LOOKAHEAD
                if n < PIECES:
                    split(n, n % RING, half)

            def normalise(s, t):
                r, ready = root_of(("x", s, t))
                dve.wait_ge(rstd_ready, ready)
                dve.tensor_scalar(work[:, t, D // 2:], x[:, t, D // 2:], r, None, ALU.mult).then_inc(xn_d, 1)

            def pre_norm(s, t, kts=range(KT)):
                for kt in kts:
                    cols, c, count = turned_cols(s, t, kt)
                    dve.wait_ge(h_hi_ready, KT * (NT * s + (t if EARLY[s] else 0)) + (kt // 2 * 2 + 2) * count)
                    dve.scalar_tensor_tensor(h_lo[:, kt, cols], ps[:, X_BANK[s] + kt // 2, c],
                                             gain(s // 3, 2 * (s % 3), kt), h_hi[:, kt, cols].bitcast(F32),
                                             ALU.mult, ALU.subtract).then_inc(h_lo_ready, count)

            def post_norm(s):
                last = BASES[s] + COUNTS[s] - 1
                for t in range(NT):
                    r, ready = root_of(("y", s, t))
                    squared = sums_before(ready - 1)
                    dve.wait_ge(g_row_in, 16 * (s + 1))
                    for b in range(2):
                        half = slice(b * D // 2, (b + 1) * D // 2)
                        dve.wait_ge(ms_ready, squared + b + 1)
                        dve.tensor_tensor(work[:, t, half], ps[:, Y_BANK[s] + 2 * t + b, :], g_row[:, half],
                                          ALU.mult).then_inc(yg_done, 1)
                    if s < 5 and t == NT - 1:
                        normalise(s + 1, 0)
                    dve.wait_ge(yg_done, 2 * (NT * s + t + 1))
                    dve.wait_ge(rstd_ready, ready)
                    for b in range(2):
                        half = slice(b * D // 2, (b + 1) * D // 2)
                        dve.scalar_tensor_tensor(x[:, t, half], work[:, t, half], r,
                                                 x[:, t, half], ALU.mult, ALU.add).then_inc(x_ready, 1)
                if s < 5:
                    early = EARLY[s + 1]
                    if not early or FILLERS[s + 1]:
                        ahead(last, 0)
                    if early:
                        pre_norm(s + 1, 0, FRONT)
                    normalise(s + 1, NT - 1)
                    if early:
                        pre_norm(s + 1, 0, BACK)
                    if not early or FILLERS[s + 1]:
                        ahead(last, 1)

            def act_mul(s, F, f, n):
                dve.wait_ge(silu_done, F + 1)
                dve.wait_ge(w_used, n + 1)
                if not isinstance(F, int) or F >= 2:
                    dve.wait_ge(a_hi_ready, F - 1)
                dve.tensor_tensor(act_f[:, f % 2, :], silu_g[:, f % 2, :], ps[:, GU_BANK[s] + 2 + f % 2, 0:SEQ],
                                  ALU.mult).then_inc(a_done, 1)

            def act_lo(F, f, slot):
                dve.wait_ge(a_hi_ready, F + 1)
                dve.tensor_tensor(a_lo[:, slot, :], act_f[:, f % 2, :], a_hi[:, slot, :].bitcast(F32),
                                  ALU.subtract).then_inc(a_lo_ready, 1)

            def mem_norm():
                for t in range(NT):
                    r, ready = root_of(("mem", 0, t))
                    dve.wait_ge(rstd_ready, ready)
                    dve.tensor_scalar(work[:, t, :], work[:, t, :], r, None,
                                      ALU.mult).then_inc(memn_ready, 1)

            def mem_gain(layer):
                for kt in range(KT):
                    dve.wait_ge(m_hi_ready, KT * layer + kt + 1)
                    dve.scalar_tensor_tensor(m_lo[:, kt, :], memT[:, kt, :], gain(layer, 6, kt),
                                             m_hi[:, kt, :].bitcast(F32), ALU.mult,
                                             ALU.subtract).then_inc(m_lo_ready, 1)

            def ffn(s):
                base, F0 = BASES[s] + FILLERS[s], FT * FFNS[s]
                ahead(base)
                act_mul(s, F0, 0, base)
                if s == 0:
                    mem_norm()
                act_lo(F0, 0, 0)
                ahead(base + 1)
                act_mul(s, F0 + 1, 1, base + 1)

                def period(c):
                    n = base + 3 * c - 1
                    F = F0 + 2 * c
                    r = (base - 1 + LOOKAHEAD) % RING
                    act_lo(F - 1, 1, 1)
                    split(n + 2, r)
                    act_mul(s, F, 0, n)
                    split(n + 3, (r + 1) % RING)
                    act_lo(F, 0, 0)
                    split(n + 4, (r + 2) % RING)
                    act_mul(s, F + 1, 1, n + 2)

                period(1)
                if s == 0:
                    mem_gain(0)
                last = FT // 2 - 1
                with dve.Fori(2, last) as c:
                    period(c)
                n = base + 3 * last - 1
                act_lo(F0 + FT - 3, 1, 1)
                ahead(n)
                act_mul(s, F0 + FT - 2, 0, n)
                act_lo(F0 + FT - 2, 0, 2)
                ahead(n + 1)
                act_mul(s, F0 + FT - 1, 1, n + 1)
                act_lo(F0 + FT - 1, 1, 3)
                ahead(n + 2)
                post_norm(s)

            def mem_values(s):
                n, b = (BASES[1] + 2, 1) if s == 1 else (BASES[3] + 1, FILL_BANK[s])
                dve.wait_ge(w_used, n)
                dve.tensor_copy(vm[:, :, :].rearrange("p a b -> p (a b)"), ps[:, b, :]).then_inc(vm_ready, 1)

            unit = [0]

            def tick(s, count=1):
                u0, units = UNITS[s]
                for i in range(unit[0], unit[0] + count):
                    if i < len(units):
                        kind, h, t = units[i]
                        u = u0 + i
                        dve.wait_ge(s_done, u + 1)
                        src = ps[:, S_BANK + i % 2, 0:SEQ]
                        if kind == "dil":
                            if i >= 2:
                                dve.wait_ge(p_done, u - 1)
                            dve.scalar_tensor_tensor(sbias[:, i % 2, :], dist[:, t, :], -(ALIBI_STEP ** (h + 1)),
                                                     ps[:, S_BANK + i % 2, :], ALU.mult, ALU.add).then_inc(sb_done, 1)
                            dve.wait_ge(sb_done, i - 2 * MEM_HEADS + 1)
                            src = sbias[:, i % 2, :]
                        dve.tensor_reduce(neg_max[:, u:u + 1], src, AX_X, ALU.max,
                                          negate=True).then_inc(max_done, 1)
                    if 3 <= i < len(units) + 3:
                        kind, h, t = units[i - 3]
                        u = u0 + i - 3
                        c = o_cols(s, kind, h)
                        dve.wait_ge(o_done, u + 1)
                        dve.wait_ge(rden_done, u + 1)
                        dve.tensor_scalar(work[:, t, c:c + HD], ps[:, O_BANK, 0:HD], rden[:, u:u + 1], None,
                                          ALU.mult).then_inc(o_ready, 1)
                    if 2 <= i < len(units) + 2:
                        u = u0 + i - 2
                        dve.wait_ge(p_done, u + 1)
                        dve.reciprocal(rden[:, u:u + 1], den[:, u:u + 1]).then_inc(rden_done, 1)
                unit[0] += count

            def beside(s, n, ticks):
                tick(s, ticks[0])
                ahead(n, 0)
                tick(s, ticks[1])
                ahead(n, 1)
                tick(s, sum(ticks[2:]))

            def out_lo(s, g):
                k = g + 1 + (4 if s == 4 else 0)
                hi, lo = ((h_hi, h_lo) if s == 1 else (m_hi, m_lo))
                hi, lo = (w[:, 2 * g:2 * g + 2, :].rearrange("p a b -> p (a b)") for w in (hi, lo))
                dve.wait_ge(oh_hi, k)
                dve.tensor_tensor(lo, ps[:, PT_BANK, :], hi.bitcast(F32), ALU.subtract).then_inc(oh_lo, 1)

            def out_los(s, n0, ticks):
                for g in range(len(ticks)):
                    beside(s, n0 + g, ticks[g][:3])
                    out_lo(s, g + 1)
                    tick(s, ticks[g][3])

            def rotate(dst, src, temp, cos, sin, done, temps):
                lo, hi = slice(0, 16), slice(16, 32)
                dve.tensor_tensor(temp[0], src, cos, ALU.mult).then_inc(temps, 1)
                dve.tensor_tensor(temp[1][:, :, lo], src[:, :, hi], sin[:, :, lo], ALU.mult).then_inc(temps, 1)
                dve.tensor_tensor(temp[1][:, :, hi], src[:, :, lo], sin[:, :, hi], ALU.mult).then_inc(temps, 1)
                rotated[0] += 3
                dve.wait_ge(temps, rotated[0])
                dve.tensor_tensor(dst, temp[0], temp[1], ALU.add).then_inc(done, 1)

            rotated = [0]

            def mixer0():
                s, base = 1, BASES[1]
                ahead(base + 1)
                mem_values(s)
                for j in range(2, 5):
                    ahead(base + j)
                for t in range(NT):
                    for kind, a, n, bank in (("cq", 0, QL, 2), ("ckv", QL, KVL, 0)):
                        r, ready = root_of((kind, 1, t))
                        dve.wait_ge(rstd_ready, ready)
                        dve.tensor_scalar(zc[:, t, a:a + n], ps[:, bank + t, 0:n], r, None,
                                          ALU.mult).then_inc(lat_ready, 1)
                dve.wait_ge(rope_ready, 2)
                t2 = [rt[:, i, 0:2 * ROPE].rearrange("p (t n) -> p t n", t=2) for i in range(2)]
                rotate(kr[:, :, :], ps[:, 2:4, QL:QL + ROPE], t2, cc[:, :, :], ss[:, :, :], kr_ready, rope_tmp)
                for c in range(5):
                    dve.wait_ge(lat_hi, min(c // 2 * 2 + 2, 5))
                    dve.scalar_tensor_tensor(m_lo[:, c, :], ps[:, 5 + c // 2, c % 2 * SEQ:(c % 2 + 1) * SEQ],
                                             gcol[:, G_Q + c:G_Q + c + 1], m_hi[:, c, :].bitcast(F32), ALU.mult,
                                             ALU.subtract).then_inc(lat_lo, 1)
                ahead(base + 5)

                def take(c):
                    is_q, half, t = chunk(c)
                    dve.wait_ge(tok_a, c + 1)
                    if is_q:
                        dve.wait_ge(tok_d, c) if c else dve.wait_ge(kr_ready, 1)
                        shape = [P, 6, ROPE]
                        rotate(tok[:, c % 4, :, NOPE:QK], tok[:, c % 4, :, NOPE:QK],
                               [rt[:, i, :].rearrange("p (h n) -> p h n", h=6) for i in range(2)],
                               cc[:, t:t + 1, :].broadcast_to(shape), ss[:, t:t + 1, :].broadcast_to(shape),
                               tok_d, rope_tmp)
                    else:
                        src = ps[:, 2 * t:2 * t + 2, 0:3 * 2 * HD].rearrange("p b (h n) -> p b h n", h=3)
                        dve.tensor_copy(v0[:, t, 6 * half:6 * half + 6, :].rearrange("p (b h) n -> p b h n", b=2),
                                        src[:, :, :, HD:2 * HD]).then_inc(tok_d, 1)

                def turned(c):
                    is_q, half, t = chunk(c)
                    dve.wait_ge(tokT_done, c + 1)
                    dst = (qT if is_q else kT)[0:QK, 6 * half:6 * half + 6, t * P:(t + 1) * P]
                    dve.tensor_scalar(dst.rearrange("p (b h) n -> p b h n", b=2),
                                      ps[0:QK, 2 * t:2 * t + 2, 0:3 * P].rearrange("p b (h n) -> p b h n", h=3),
                                      QK ** -0.5 if is_q else 1.0, None, ALU.mult).then_inc(tokT_d, 1)

                for piece, ticks in enumerate(TICKS0):
                    beside(s, base + 6 + piece, ticks[:2])
                    take(2 * piece)
                    tick(s, ticks[2])
                    take(2 * piece + 1)
                    tick(s, ticks[3] + ticks[4])
                    turned(2 * piece + 1)
                    if piece == 3:
                        out_lo(s, 0)
                    tick(s, ticks[5])
                mem_gain(1)
                out_los(s, base + 10, TICKS0_OUT)
                post_norm(s)

            def mixer1():
                s, base = 4, BASES[4]
                ahead(base)
                for j, (kind, g, p) in enumerate(STEPS1):
                    n, b = base + 1 + j, (1 + j) % 4
                    if j < len(STEPS1) - 1:
                        beside(s, n, TICKS1[j])
                    else:
                        beside(s, n, TICKS1[j][:3])
                        out_lo(s, 0)
                        tick(s, TICKS1[j][3])
                    if j % 2 == 1:
                        dve.wait_ge(w_used, n + 1)
                        if kind == "qk":
                            dve.tensor_scalar(q1T[:, g, p, :], ps[:, b, 0:SEQ], HD ** -0.5, None,
                                              ALU.mult).then_inc(z1_d, 1)
                            dve.tensor_copy(k1T[:, g, p, :], ps[:, b, SEQ:2 * SEQ]).then_inc(z1_d, 1)
                        else:
                            dst, src = value_rows(kind, p, b)
                            dve.tensor_copy(dst, src).then_inc(z1_d, 1)
                out_los(s, base + 19, TICKS1_OUT)
                post_norm(s)

            for t in range(NT):
                normalise(0, t)
            dve.wait_ge(gcol_in, 16)
            pre_norm(0, 0)
            split(0, 0, 0)
            for s in range(6):
                if s == 1:
                    ahead(BASES[s])
                pre_norm(s, NT - 1)
                if s == 0:
                    split(0, 0, 1)
                    split(1, 1)
                elif FILLERS[s] == 1:
                    ahead(BASES[s])
                    if s == 3:
                        mem_values(s)
                elif EARLY[s]:
                    ahead(BASES[s] - 1)
                unit[0] = 0
                if s == 1:
                    mixer0()
                elif s == 4:
                    mixer1()
                else:
                    ffn(s)

        @block.tensor
        def _(pe):
            def arrived(n):
                pe.wait_ge(lo_ready, 2 * n + 2)

            def triple(out_ap, st_hi, st_lo, mv_hi, mv_lo, start, stop):
                pe.matmul(out_ap, st_hi, mv_hi, start=start, stop=False)
                pe.matmul(out_ap, st_hi, mv_lo, start=False, stop=False)
                return pe.matmul(out_ap, st_lo, mv_hi, start=False, stop=stop)

            def weights(slot):
                return (w[:, slot, :].rearrange("p (k n) -> p k n", k=KT) for w in (w_hi, w_lo))

            def keep_clock(bank, count):
                for _ in range(count):
                    pe.matmul(ps[:, bank, 0:P], ident, ident, start=True, stop=True)

            def pre_norm(s, t):
                keep_clock(*IDLE[s][t])
                for kt in range(KT):
                    if kt % (KT // 2) == 0:
                        pe.wait_ge((xn_a, xn_d)[kt // (KT // 2)], NT * s + t + 1)
                    if kt % 2 == 0 and t:
                        if EARLY[s]:
                            pe.wait_ge(h_lo_ready, KT * NT * s + kt + 2)
                    c = kt % 2 * SEQ + t * P
                    last = pe.transpose(ps[:, X_BANK[s] + kt // 2, c:c + P],
                                        work[:, t, kt * P:(kt + 1) * P], ident)
                    if kt % 2:
                        last.then_inc(xT_done, 1)

            def gate_up(s, F, f, n, slot, first=False):
                if not isinstance(F, int) or F >= 2:
                    pe.wait_ge(a_done, F - 1)
                for half in range(2):
                    pe.wait_ge(lo_ready, 2 * n + 1 + half)
                    wh, wl = (w[:, slot, half * 1024:(half + 1) * 1024].rearrange("p (k n) -> p k n", k=KT)
                              for w in (w_hi, w_lo))
                    for kt in range(KT):
                        if first and half == 0:
                            pe.wait_ge(h_lo_ready, KT * (NT * s + 1) + kt + 1)
                        last = triple(ps[:, GU_BANK[s] + 2 * half + f % 2, 0:SEQ], wh[:, kt, :], wl[:, kt, :],
                                      h_hi[:, kt, :], h_lo[:, kt, :], kt == 0, kt == KT - 1)
                    last.then_inc((g_done, w_used)[half], 1)

            def quarter(s, slot, src_hi, src_lo, row, j, t, first, last, halves=(0, 1)):
                sh, sl = src_hi[:, row, t * P:(t + 1) * P], src_lo[:, row, t * P:(t + 1) * P]
                for k, (st, w) in enumerate(((sh, w_hi), (sh, w_lo), (sl, w_hi))):
                    for half in halves:
                        c = j * 1024 + half * 512
                        ins = pe.matmul(ps[:, Y_BANK[s] + 2 * t + half, :], st, w[:, slot, c:c + 512],
                                        start=first and k == 0, stop=last and k == 2)
                return ins

            def mem_transposes():
                pe.wait_ge(memn_ready, NT)
                for kt in range(KT):
                    for t in range(NT):
                        c = kt % 2 * NMEM + t * P
                        last = pe.transpose(ps[:, kt // 2, c:c + P], work[:, t, kt * P:(kt + 1) * P], ident)
                last.then_inc(memT_done, 1)

            def ffn(s):
                base, F0 = BASES[s] + FILLERS[s], FT * FFNS[s]
                gate_up(s, F0, 0, base, base % RING, first=True)
                if s == 2:
                    pe.wait_ge(km_ready, 2)
                if s == 3:
                    pe.wait_ge(vm_ready, 2)
                gate_up(s, F0 + 1, 1, base + 1, (base + 1) % RING)
                if s == 0:
                    mem_transposes()

                def period(c, first=False):
                    n = base + 3 * c - 1
                    F = F0 + 2 * c
                    r = (base - 1) % RING
                    gate_up(s, F, 0, n, r)
                    if first and s == 0:
                        pe.wait_ge(memT_ready, KT // 2)
                    arrived(n + 1)
                    pe.wait_ge(a_lo_ready, F)
                    for j in range(2):
                        for t in range(NT):
                            last = quarter(s, (r + 1) % RING, a_hi, a_lo, j, j, t, first and j == 0, False)
                    last.then_inc(w_used, 1)
                    gate_up(s, F + 1, 1, n + 2, (r + 2) % RING)

                period(1, first=True)
                last = FT // 2 - 1
                with pe.Fori(2, last) as c:
                    period(c)
                n = base + 3 * last - 1
                gate_up(s, F0 + FT - 2, 0, n, n % RING)
                gate_up(s, F0 + FT - 1, 1, n + 1, (n + 1) % RING)
                for t in range(NT):
                    for b in range(2):
                        for piece in range(2):
                            if t == b == 0:
                                arrived(n + 2 + piece)
                                pe.wait_ge(a_lo_ready, F0 + FT - 2 + 2 * piece)
                            for j in range(2):
                                ins = quarter(s, (n + 2 + piece) % RING, a_hi, a_lo, 2 * piece + j, j, t, False,
                                              piece == j == 1, (b,))
                            if t == b == 1:
                                ins.then_inc(w_used, 1)
                        if not t == b == 1:
                            ins.then_inc(y_done, 1)

            def columns(slot, out_ap, src_hi, src_lo):
                wh, wl = weights(slot)
                for m in range(2):
                    for kt in range(KT):
                        last = triple(out_ap[:, m * SEQ:(m + 1) * SEQ], wh[:, kt, m * P:(m + 1) * P],
                                      wl[:, kt, m * P:(m + 1) * P], src_hi[:, kt, :], src_lo[:, kt, :],
                                      kt == 0, kt == KT - 1)
                        if kt == KT // 2 - 1:
                            yield
                    if m == 1:
                        last.then_inc(w_used, 1)
                    yield

            def rows(slot, outs, width, src_hi, src_lo):
                wh, wl = weights(slot)
                for t in range(NT):
                    for kt in range(KT):
                        last = triple(outs[t], src_hi[:, kt, t * P:(t + 1) * P], src_lo[:, kt, t * P:(t + 1) * P],
                                      wh[:, kt, 0:width], wl[:, kt, 0:width], kt == 0, kt == KT - 1)
                        if kt == KT // 2 - 1:
                            yield
                    if t == NT - 1:
                        last.then_inc(w_used, 1)
                    yield

            def run(product):
                for _ in product:
                    pass

            def filler(s, product):
                for q, _ in enumerate(product):
                    if q == 1 and EARLY[s]:
                        pre_norm(s, 0)

            def y_read(s):
                pe.wait_ge(yg_done, 2 * NT * s + 2)
                pe.wait_ge(ms_ready, sums_before(SQUARES.index(("y", s, 0))) + 2)

            def memory_keys(s):
                arrived(BASES[s])
                pe.wait_ge(m_lo_ready, KT * (2 if s > 1 else 1))
                y_read(s - 1)
                filler(s, columns(BASES[s] % RING, ps[:, FILL_BANK[s], :], m_hi, m_lo))

            def memory_values(s):
                n, b = (BASES[1] + 1, 1) if s == 1 else (BASES[3], FILL_BANK[s])
                arrived(n)
                if s == 3:
                    y_read(s - 1)
                product = rows(n % RING, [ps[:, b, t * 256:(t + 1) * 256] for t in range(2)], 256, m_hi, m_lo)
                if s == 3:
                    filler(s, product)
                else:
                    run(product)

            unit = [0]
            pt_free = [None]

            def tick(s, count=1):
                u0, units = UNITS[s]
                for i in range(unit[0], unit[0] + count):
                    if i < len(units):
                        kind, h, t = units[i]
                        tok_cols = slice(t * P, (t + 1) * P)
                        if i >= 2:
                            pe.wait_ge(p_done, u0 + i - 1)
                        bank = ps[:, S_BANK + i % 2, :]
                        if kind == "mla":
                            if h % (MLA_HEADS // 2) == t == 0:
                                for turned in (tokT_a, tokT_d):
                                    pe.wait_ge(turned, 2 * (h // (MLA_HEADS // 2)) + 2)
                            last = pe.matmul(bank[:, 0:SEQ], qT[0:QK, h, tok_cols], kT[0:QK, h, :],
                                             start=True, stop=True)
                        else:
                            pr = slice(h % 2 * HD, (h % 2 + 1) * HD)
                            if kind == "mem":
                                last = pe.matmul(bank[:, 0:SEQ], qmT[pr, h // 2, tok_cols], kmT[pr, h // 2, :],
                                                 start=True, stop=True)
                            else:
                                if h % 2 == t == 0:
                                    for k in range(3):
                                        pe.wait_ge(*evacuated(STEPS1.index(("qk", k, h // 2))))
                                pe.matmul(bank[:, 0:SEQ], q1T[pr, 0, h // 2, tok_cols], k1T[pr, 0, h // 2, :],
                                          start=True, stop=True)
                                for g in (1, 2):
                                    last = pe.matmul(bank[:, SEQ + (g - 1) * P:SEQ + g * P],
                                                     q1T[pr, g, h // 2, tok_cols], k1T[pr, g, h // 2, tok_cols],
                                                     start=True, stop=True)
                        last.then_inc(s_done, 1)
                    if 2 <= i < len(units) + 2:
                        kind, h, t = units[i - 2]
                        j = i - 2
                        pe.wait_ge(p_done, u0 + j + 1)
                        if pt_free[0]:
                            pe.wait_ge(*pt_free[0])
                        for c in range(4 if kind == "dil" else 2):
                            last = pe.transpose(ps[:, PT_BANK, c * P:(c + 1) * P],
                                                prob[:, j % 2, c * P:(c + 1) * P], ident)
                        last.then_inc(pT_done, 1)
                        pt_free[0] = (pT_ready, u0 + j + 1)
                    if 3 <= i < len(units) + 3:
                        kind, h, t = units[i - 3]
                        j = i - 3
                        pe.wait_ge(pT_ready, u0 + j + 1)
                        if u0 + j:
                            pe.wait_ge(o_ready, u0 + j)
                        hc = slice(h * HD, (h + 1) * HD)
                        if kind == "dil":
                            if h % 2 == t == 0:
                                pe.wait_ge(*evacuated(STEPS1.index(("v01", 0, h // 2))))
                                pe.wait_ge(*evacuated(STEPS1.index(("v2", 2, h // 4 * 2))))
                            vals = [v1[:, 0, 0, hc], v1[:, 0, 1, hc], v1[:, 1, t, hc], v1[:, 2, t, hc]]
                        elif kind == "mla":
                            vals = [v0[:, c, h, :] for c in range(2)]
                        else:
                            vals = [vm[:, c, hc] for c in range(2)]
                        for c, v in enumerate(vals):
                            last = pe.matmul(ps[:, O_BANK, 0:HD], probT[:, j % 2, c * P:(c + 1) * P], v,
                                             start=c == 0, stop=c == len(vals) - 1)
                        last.then_inc(o_done, 1)
                unit[0] += count

            def turn_out(s, g):
                k0, needed = out_groups(s)[g]
                pe.wait_ge(o_ready, UNITS[s][0] + needed)
                pe.wait_ge(*pt_free[0])
                for k in range(2):
                    for t in range(NT):
                        c = k * SEQ + t * P
                        last = pe.transpose(ps[:, PT_BANK, c:c + P],
                                            work[:, t, (k0 + k) * P:(k0 + k + 1) * P], ident)
                last.then_inc(oT_done, 1)
                pt_free[0] = (oh_lo, g + 1 + (4 if s == 4 else 0))

            def project(s, n0, ticks):
                groups = len(ticks) + 1
                src_hi, src_lo = (h_hi, h_lo) if s == 1 else (m_hi, m_lo)
                for g in range(groups):
                    arrived(n0 + g)
                    pe.wait_ge(oh_lo, g + 1 + (4 if s == 4 else 0))
                    if g == groups - 1:
                        for q in range(4):
                            t, b = q // 2, q % 2
                            for j in range(2):
                                last = quarter(s, (n0 + g) % RING, src_hi, src_lo, 2 * g + j, j, t, False, j == 1,
                                               (b,))
                            last.then_inc((y_done, w_used)[q == 3], 1)
                        continue
                    for q in range(4):
                        j, t = (q % 2, q // 2) if g == 0 else (q // 2, q % 2)
                        if s == 4 and g == 0 and j == 0:
                            for k in ((15, 16), (14, 17))[t]:
                                pe.wait_ge(*evacuated(k))
                        last = quarter(s, (n0 + g) % RING, src_hi, src_lo, 2 * g + j, j, t, g == 0 and j == 0, False)
                        if q == 3:
                            last.then_inc(w_used, 1)
                        tick(s, ticks[g][q])
                        if q == 2:
                            turn_out(s, g + 1)

            def mixer0():
                s, base = 1, BASES[1]
                pe.wait_ge(h_lo_ready, KT * NT * (s + 1))
                arrived(base + 2)
                run(rows((base + 2) % RING, [ps[:, 2 + t, 0:256] for t in range(NT)], 256, h_hi, h_lo))
                arrived(base + 3)
                run(rows((base + 3) % RING, [ps[:, 2 + t, 256:256 + P + ROPE] for t in range(NT)], P + ROPE,
                         h_hi, h_lo))
                arrived(base + 4)
                pe.wait_ge(km_ready, 1)
                pe.wait_ge(vm_ready, 1)
                run(rows((base + 4) % RING, [ps[:, t, 0:256] for t in range(NT)], 256, h_hi, h_lo))
                arrived(base + 5)
                for q, _ in enumerate(columns((base + 5) % RING, ps[:, 4, :], h_hi, h_lo)):
                    if q == 2:
                        for t in range(NT):
                            pe.wait_ge(lat_ready, 2 * t + 2)
                            for c in range(5):
                                o = c % 2 * SEQ + t * P
                                last = pe.transpose(ps[:, 5 + c // 2, o:o + P],
                                                    zc[:, t, c * P:(c + 1) * P], ident)
                        last.then_inc(latT_done, 1)
                pt_free[0] = (lat_lo, 5)

                def turn(c):
                    is_q, half, t = chunk(c)
                    pe.wait_ge(tok_a, c + 1)
                    pe.wait_ge(tok_d, c + 1)
                    if not is_q:
                        pe.wait_ge(tok_p, 2 * half + t + 1)
                    for h in range(6):
                        last = pe.transpose(ps[0:QK, 2 * t + h // 3, h % 3 * P:(h % 3 + 1) * P],
                                            tok[:, c % 4, h, :], ident)
                    last.then_inc(tokT_done, 1)

                for piece in range(4):
                    n = base + 6 + piece
                    arrived(n)
                    kts, k0, width = (3, 0, 3 * QK) if piece % 2 == 0 else (2, 3, 3 * 2 * HD)
                    for t in range(NT):
                        c = 2 * piece + t
                        if c == 1:
                            pe.wait_ge(kr_ready, 1)
                        if c >= 2:
                            pe.wait_ge((tokT_a, tokT_d)[t], piece)
                        for b in range(2):
                            if t or b:
                                if piece == t == 0:
                                    pe.wait_ge(qm_ready, 1)
                                tick(s, TICKS0[piece][2 * t + b - 1])
                            for k in range(kts):
                                if piece < 2 and t == b == 0:
                                    pe.wait_ge(lat_lo, k0 + k + 1)
                                o = k * 2 * width + b * width
                                last = triple(ps[:, 2 * t + b, 0:width], m_hi[:, k0 + k, t * P:(t + 1) * P],
                                              m_lo[:, k0 + k, t * P:(t + 1) * P], w_hi[:, n % RING, o:o + width],
                                              w_lo[:, n % RING, o:o + width], k == 0, k == kts - 1)
                        last.then_inc((up_done, w_used)[t], 1)
                    tick(s, TICKS0[piece][3])
                    turn(2 * piece)
                    tick(s, TICKS0[piece][4])
                    turn(2 * piece + 1)
                    if piece == 3:
                        turn_out(s, 0)
                    tick(s, TICKS0[piece][5])
                project(s, base + 10, TICKS0_OUT)

            def mixer1():
                s, base = 4, BASES[4]
                pe.wait_ge(h_lo_ready, KT * NT * (s + 1))
                arrived(base)
                run(columns(base % RING, ps[:, 0, :], h_hi, h_lo))
                for k, (kind, g, p) in enumerate(STEPS1):
                    n, b = base + 1 + k, (1 + k) % 4
                    arrived(n)
                    if k == 0:
                        pe.wait_ge(qm_ready, 2)
                        pe.wait_ge(vm_ready, 2)
                        pe.wait_ge(km_ready, 2)
                    if k >= 4:
                        pe.wait_ge(*evacuated(k - 4))
                    if kind == "qk":
                        product = columns(n % RING, ps[:, b, :], h_hi, h_lo)
                    else:
                        product = rows(n % RING, [ps[:, b, t * 256:(t + 1) * 256] for t in range(NT)], 256,
                                       h_hi, h_lo)
                    for q, _ in enumerate(product):
                        if q == 3 and k == len(STEPS1) - 1:
                            turn_out(s, 0)
                        tick(s, TICKS1[k][q])
                project(s, base + 19, TICKS1_OUT)

            for s in range(6):
                unit[0] = 0
                if s in (1, 2):
                    memory_keys(s)
                if s == 3:
                    memory_values(s)
                if s == 0:
                    pe.wait_ge(ident_in, 16)
                if not (FILLERS[s] and EARLY[s]):
                    pre_norm(s, 0)
                pre_norm(s, NT - 1)
                keep_clock(*IDLE[s][NT])
                if s == 1:
                    memory_values(s)
                    mixer0()
                elif s == 4:
                    mixer1()
                else:
                    ffn(s)


ROPE_STEPS = 1 + NT + 5 + 12 + 1 + 4


def _token_order():
    return np.arange(SEQ).reshape(SEQ // CLASSES, CLASSES).T.reshape(-1)


def _constants():
    token = _token_order()
    diff = np.abs(token[:, None] - token[None, :])
    table = []
    for g, (window, dil) in enumerate(GROUPS):
        seen = (diff % dil == 0) & (diff // dil <= window // (2 * dil))
        d = np.where(seen, diff * ALIBI_STEP ** (8 * g), MASKED)
        table.append(d)
    rows = []
    for t in range(NT):
        own = slice(t * P, (t + 1) * P)
        assert all((table[g][own, :P * NT].min(1) < MASKED).all() for g in range(3))
        rows.append(np.concatenate([table[0][own, :], table[1][own, own], table[2][own, own]], axis=1))
    dist = np.stack(rows, 1).reshape(P, -1)
    inv = np.float32(10000.0) ** (-np.arange(16, dtype=np.float32) / np.float32(16))
    return np.concatenate([np.eye(P), dist, np.broadcast_to(inv, (P, 16))], axis=1).astype(np.float32)


def _by_columns(w, cols):
    w = w[:, cols]
    k = w.shape[0] // P
    w = w.reshape(k, P, w.shape[1]).transpose(1, 0, 2)
    if k == KT and w.shape[2] < PIECE // KT:
        w = np.concatenate([w, np.zeros((P, k, PIECE // KT - w.shape[2]), w.dtype)], axis=2)
    w = w.reshape(P, -1)
    return np.concatenate([w, np.zeros((P, PIECE - w.shape[1]), w.dtype)], axis=1)


def _by_rows(w, kt):
    return w[kt * P:(kt + 2) * P].reshape(2, P, D).transpose(1, 0, 2).reshape(P, PIECE)


def _stream(a):
    pieces = []

    def ffn(l, i):
        wg, wu, wd = a["ffn_w_gate"][l, i], a["ffn_w_up"][l, i], a["ffn_w_down"][l, i]

        def gate_up(f):
            cols = slice(f * P, (f + 1) * P)
            pieces.append(np.concatenate(
                [w[:, cols].reshape(KT, P, P).transpose(1, 0, 2).reshape(P, -1) for w in (wg, wu)], axis=1))

        gate_up(0)
        gate_up(1)
        for c in range(1, FT // 2 - 1):
            gate_up(2 * c)
            pieces.append(_by_rows(wd, 2 * c - 2))
            gate_up(2 * c + 1)
        gate_up(FT - 2)
        gate_up(FT - 1)
        pieces.append(_by_rows(wd, FT - 4))
        pieces.append(_by_rows(wd, FT - 2))

    def memory(l, c):
        pieces.append(_by_columns(a["mem_w_kv"][l], slice(c * 256, (c + 1) * 256)))

    def out(w):
        n = w.shape[0] // P - 2
        for kt in (n, *range(0, n, 2)):
            pieces.append(_by_rows(w, kt))

    ffn(0, 0)
    memory(0, 0)
    memory(0, 1)
    w = a["a_w_in"][0]
    o2, o3 = QL + KVL, QL + KVL + ROPE
    pieces.append(_by_columns(w, slice(0, 256)))
    pieces.append(_by_columns(w, np.r_[256:QL, o2:o3]))
    pieces.append(_by_columns(w, slice(QL, o2)))
    pieces.append(_by_columns(w, slice(o3, o3 + 256)))
    for half in range(2):
        for w, n in ((a["a_w_uq"][0], QK), (a["a_w_ukv"][0], 2 * HD)):
            pieces.append(_by_columns(w, slice(half * 6 * n, (half + 1) * 6 * n)))
    out(a["a_w_out"][0])
    memory(1, 0)
    ffn(0, 1)
    memory(1, 1)
    ffn(1, 0)
    w = a["b_w_in"][0]
    width = DIL_HEADS * HD
    own = 3 * 3 * width
    pieces.append(_by_columns(w, slice(own, own + MEM_HEADS * HD)))

    def cols(g, which, p, pairs=1):
        c = (3 * g + which) * width + p * P
        return np.arange(c, c + pairs * P)

    for kind, g, p in STEPS1:
        if kind == "qk":
            c = np.concatenate([cols(g, 0, p), cols(g, 1, p)])
        elif kind == "v01":
            c = np.concatenate([cols(0, 2, p), cols(1, 2, p)])
        else:
            c = cols(2, 2, p, 2)
        pieces.append(_by_columns(w, c))
    out(a["b_w_out"][0])
    ffn(1, 1)
    assert len(pieces) == PIECES
    return np.stack(pieces)


def kernel(**inputs):
    from concourse import bacc
    from concourse.bass_utils import run_bass_kernel_spmd

    a = {k: np.asarray(v) for k, v in inputs.items()}
    order = _token_order()
    norm_g = a["norm_g"]
    arrays = {
        "x_in": a["x"][0][order].reshape(NT, P, D),
        "mem_in": a["mem"][0].reshape(NT, P, D),
        "pos_in": a["positions"][0][order].reshape(NT, P).T,
        "stream": _stream(a),
        "gcols": np.concatenate([norm_g.reshape(2 * 7 * KT, P).T, a["a_q_norm"].reshape(-1, P).T,
                                 a["a_kv_norm"].reshape(-1, P).T], axis=1),
        "grows": norm_g[:, [1, 3, 5]].reshape(6, D),
        "consts": _constants(),
    }
    arrays = {k: np.ascontiguousarray(v) for k, v in arrays.items()}
    nc = bacc.Bacc("TRN2", target_bir_lowering=False, num_devices=1)
    args = [nc.dram_tensor(k, v.shape, mybir.dt.from_np(v.dtype), kind="ExternalInput").ap()
            for k, v in arrays.items()]
    args.append(nc.dram_tensor("out", (NT, P, D), F32, kind="ExternalOutput").ap())
    build(nc, *args)
    r = run_bass_kernel_spmd(nc, [arrays], core_ids=[0])
    got = r.results[0]["out"].reshape(SEQ, D)
    back = np.argsort(order)
    return got[back].reshape(1, SEQ, D)
```
